# Optimizing a Trainium2 kernel written in Bass

```python
import jax, jax.numpy as jnp
from jax import lax
import numpy as np
import math

D_MODEL = 1024
BATCH = 1
SEQ = 512
DEPTH = 2

N_META = 16
BLOCK = 128
META_PAD = BLOCK - N_META
RMS_EPS = 1e-6
NEG_INF = -1e30

LRU_WIDTH = D_MODEL // 2
LRU_HEADS = 8
LRU_BLOCK_W = LRU_WIDTH // LRU_HEADS
CONV_W = 4
LRU_C = 8.0

ATT_HEADS = 8
ATT_KV_HEADS = 2
ATT_HEAD_DIM = 64
WINDOW = 128
ROPE_THETA = 500000.0
ROT_DIM = ATT_HEAD_DIM // 4
Q_WIDTH = ATT_HEADS * ATT_HEAD_DIM
KV_WIDTH = ATT_KV_HEADS * ATT_HEAD_DIM
AB_IN_WIDTH = 2 * LRU_WIDTH + Q_WIDTH + 2 * KV_WIDTH
AB_OUT_WIDTH = LRU_WIDTH + Q_WIDTH
SPLIT_AB = (LRU_WIDTH, 2 * LRU_WIDTH, 2 * LRU_WIDTH + Q_WIDTH, 2 * LRU_WIDTH + Q_WIDTH + KV_WIDTH)

RET_HEADS = 4
RET_QK_DIM = D_MODEL // RET_HEADS
RET_V_DIM = 2 * D_MODEL // RET_HEADS
RET_THETA = 10000.0
RET_IN_WIDTH = 6 * D_MODEL
SPLIT_RET = (D_MODEL, 2 * D_MODEL, 4 * D_MODEL)

D_FF = -(-8 * D_MODEL // (3 * 256)) * 256


F32 = jnp.float32

def _rmsnorm(x, gain):
    xf = x.astype(F32)
    y = xf * lax.rsqrt(jnp.mean(xf * xf, axis=-1, keepdims=True) + RMS_EPS)
    return (y * gain.astype(F32)).astype(x.dtype)

def _rms_noaffine(x):
    xf = x.astype(F32)
    return xf * lax.rsqrt(jnp.mean(xf * xf, axis=-1, keepdims=True) + RMS_EPS)

def _rope_tables(n_pos, rot_dim, theta):
    half = rot_dim // 2
    inv_freq = jnp.power(jnp.asarray(theta, F32), -jnp.arange(half, dtype=F32) / half)
    ang = jnp.arange(n_pos, dtype=F32)[:, None] * inv_freq[None, :]
    return jnp.cos(ang), jnp.sin(ang)

def _rotary(x, cos, sin):
    half = cos.shape[-1]
    c = cos[None, :, None, :]
    s = sin[None, :, None, :]
    x1 = x[..., :half].astype(F32)
    x2 = x[..., half:2 * half].astype(F32)
    rot = jnp.concatenate([x1 * c - x2 * s, x2 * c + x1 * s], axis=-1).astype(x.dtype)
    return jnp.concatenate([rot, x[..., 2 * half:]], axis=-1)

def _rg_lru(xr, conv_w, conv_b, w_a, b_a, w_i, b_i, lam):
    B, T, W = xr.shape
    xp = jnp.pad(xr, ((0, 0), (CONV_W - 1, 0), (0, 0)))
    xc = sum((xp[:, j:j + T, :] * conv_w[j] for j in range(CONV_W)), conv_b)
    xh = xc.reshape(B, T, LRU_HEADS, LRU_BLOCK_W)
    r = jax.nn.sigmoid((jnp.einsum('bthi,hij->bthj', xh, w_a) + b_a).astype(F32)).reshape(B, T, W)
    i = jax.nn.sigmoid((jnp.einsum('bthi,hij->bthj', xh, w_i) + b_i).astype(F32)).reshape(B, T, W)
    log_a = -LRU_C * r * jax.nn.softplus(-lam.astype(F32))
    a = jnp.exp(log_a)
    mult = jnp.sqrt(-jnp.expm1(2.0 * log_a))
    mult = jnp.where(jnp.arange(T)[None, :, None] == 0, 1.0, mult)
    b = mult * i * xc.astype(F32)

    def combine(left, right):
        a_l, b_l = left
        a_r, b_r = right
        return a_l * a_r, a_r * b_l + b_r

    _, h = lax.associative_scan(combine, (a, b), axis=1)
    return h.astype(xr.dtype)

def _swa_with_sinks(q, k, v, sinks):
    B, T, Hq, Dh = q.shape
    G = ATT_HEADS // ATT_KV_HEADS
    Tp = T + META_PAD
    NB = Tp // BLOCK
    qb = jnp.pad(q, ((0, 0), (META_PAD, 0), (0, 0), (0, 0))).reshape(B, NB, BLOCK, ATT_KV_HEADS, G, Dh)
    kpad = ((0, 0), (META_PAD + BLOCK, 0), (0, 0), (0, 0))
    kb = jnp.pad(k, kpad).reshape(B, NB + 1, BLOCK, ATT_KV_HEADS, Dh)
    vb = jnp.pad(v, kpad).reshape(B, NB + 1, BLOCK, ATT_KV_HEADS, Dh)
    k_win = jnp.concatenate([kb[:, :-1], kb[:, 1:]], axis=2)
    v_win = jnp.concatenate([vb[:, :-1], vb[:, 1:]], axis=2)
    k_meta = k[:, :N_META]
    v_meta = v[:, :N_META]
    scale = Dh ** -0.5
    s_meta = jnp.einsum('bnqhgd,bkhd->bnhgqk', qb, k_meta)
    s_win = jnp.einsum('bnqhgd,bnkhd->bnhgqk', qb, k_win)
    s = jnp.concatenate([s_meta, s_win], axis=-1).astype(F32) * scale
    nb = jnp.arange(NB)[:, None]
    qpos = nb * BLOCK + jnp.arange(BLOCK)[None, :] - META_PAD
    kpos = (nb - 1) * BLOCK + jnp.arange(2 * BLOCK)[None, :] - META_PAD
    qp = qpos[:, :, None]
    kp = kpos[:, None, :]
    win_mask = (kp >= N_META) & (kp <= qp) & (qp - kp < WINDOW)
    meta_mask = jnp.arange(N_META)[None, None, :] <= qp
    mask = jnp.concatenate([meta_mask, win_mask], axis=-1)
    s = jnp.where(mask[None, :, None, None], s, NEG_INF)
    sink = jnp.broadcast_to(sinks.astype(F32).reshape(1, 1, ATT_KV_HEADS, G, 1, 1), s.shape[:-1] + (1,))
    p = jax.nn.softmax(jnp.concatenate([s, sink], axis=-1), axis=-1)[..., :-1].astype(v.dtype)
    o = (jnp.einsum('bnhgqk,bkhd->bnqhgd', p[..., :N_META], v_meta)
         + jnp.einsum('bnhgqk,bnkhd->bnqhgd', p[..., N_META:], v_win))
    return o.reshape(B, Tp, Hq * Dh)[:, META_PAD:]

def _mixer_rglru_swa(h, cos, sin, w_in, conv_w, conv_b, w_a, b_a, w_i, b_i, lam,
                     q_gain, k_gain, sinks, w_out):
    B, T, _ = h.shape
    x_rnn, gate, q, k, v = jnp.split(h @ w_in, SPLIT_AB, axis=-1)
    y_rnn = jax.nn.gelu(gate) * _rg_lru(x_rnn, conv_w, conv_b, w_a, b_a, w_i, b_i, lam)
    q = _rotary(_rmsnorm(q.reshape(B, T, ATT_HEADS, ATT_HEAD_DIM), q_gain), cos, sin)
    k = _rotary(_rmsnorm(k.reshape(B, T, ATT_KV_HEADS, ATT_HEAD_DIM), k_gain), cos, sin)
    v = v.reshape(B, T, ATT_KV_HEADS, ATT_HEAD_DIM)
    y_att = _swa_with_sinks(q, k, v, sinks)
    return jnp.concatenate([y_rnn, y_att], axis=-1) @ w_out

def _mixer_retention(h, cos, sin, w_in, w_out):
    B, T, _ = h.shape
    q, k, v, g = jnp.split(h @ w_in, SPLIT_RET, axis=-1)
    q = _rotary(q.reshape(B, T, RET_HEADS, RET_QK_DIM), cos, sin)
    k = _rotary(k.reshape(B, T, RET_HEADS, RET_QK_DIM), cos, sin) * (RET_QK_DIM ** -0.5)
    v = v.reshape(B, T, RET_HEADS, RET_V_DIM)
    Tp = T + META_PAD
    NC = Tp // BLOCK

    def to_chunks(t):
        d = t.shape[-1]
        t = jnp.pad(t, ((0, 0), (META_PAD, 0), (0, 0), (0, 0)))
        return t.reshape(B, NC, BLOCK, RET_HEADS, d).transpose(1, 0, 3, 2, 4)

    qc, kc, vc = to_chunks(q), to_chunks(k), to_chunks(v)
    log_g = jnp.log1p(-jnp.exp2(-5.0 - jnp.arange(RET_HEADS, dtype=F32)))
    idx = jnp.arange(BLOCK, dtype=F32)
    diff = idx[:, None] - idx[None, :]
    decay_intra = jnp.where(diff >= 0, jnp.exp(jnp.maximum(diff, 0.0)[None] * log_g[:, None, None]), 0.0)
    decay_q = jnp.exp((idx + 1.0)[None] * log_g[:, None])
    decay_k = jnp.exp((BLOCK - 1.0 - idx)[None] * log_g[:, None])
    decay_chunk = jnp.exp(BLOCK * log_g)

    def step(state, chunk):
        qn, kn, vn = chunk
        vf = vn.astype(F32)
        qk = jnp.einsum('bhid,bhjd->bhij', qn, kn).astype(F32) * decay_intra
        o = (jnp.einsum('bhij,bhjv->bhiv', qk, vf)
             + jnp.einsum('bhid,bhdv->bhiv', qn.astype(F32) * decay_q[..., None], state))
        state = (decay_chunk[:, None, None] * state
                 + jnp.einsum('bhjd,bhjv->bhdv', kn.astype(F32) * decay_k[..., None], vf))
        return state, o

    state0 = jnp.zeros((B, RET_HEADS, RET_QK_DIM, RET_V_DIM), F32)
    _, o = lax.scan(step, state0, (qc, kc, vc))
    o = o.transpose(1, 0, 3, 2, 4).reshape(B, Tp, RET_HEADS, RET_V_DIM)[:, META_PAD:]
    o = _rms_noaffine(o).reshape(B, T, 2 * D_MODEL).astype(h.dtype)
    return (jax.nn.silu(g) * o) @ w_out

def _swiglu(h, w_gu, w_down):
    gate, up = jnp.split(h @ w_gu, 2, axis=-1)
    return (jax.nn.silu(gate) * up) @ w_down

def first_inputs(seed: int = 0) -> dict:
    key = jax.random.key(seed)
    keys = jax.random.split(key, 24)
    n_even = (DEPTH + 1) // 2
    n_odd = DEPTH // 2

    def normal(k, shape, scale):
        return jax.random.normal(k, shape, F32) * scale

    def gain(k, shape):
        return 1.0 + 0.02 * jax.random.normal(k, shape, F32)

    u = jax.random.uniform(keys[10], (n_even, LRU_WIDTH), F32, minval=0.9, maxval=0.999)
    a = u ** (1.0 / LRU_C)
    lam = jnp.log(a) - jnp.log1p(-a)
    return {
        'x': normal(keys[0], (BATCH, SEQ, D_MODEL), 1.0),
        'meta_tokens': normal(keys[1], (N_META, D_MODEL), 1.0),
        'mix_norm_ab': gain(keys[2], (n_even, D_MODEL)),
        'ab_w_in': normal(keys[3], (n_even, D_MODEL, AB_IN_WIDTH), D_MODEL ** -0.5),
        'lru_conv_w': normal(keys[4], (n_even, CONV_W, LRU_WIDTH), CONV_W ** -0.5),
        'lru_conv_b': normal(keys[5], (n_even, LRU_WIDTH), 0.01),
        'lru_w_a': normal(keys[6], (n_even, LRU_HEADS, LRU_BLOCK_W, LRU_BLOCK_W), LRU_BLOCK_W ** -0.5),
        'lru_b_a': normal(keys[7], (n_even, LRU_HEADS, LRU_BLOCK_W), 0.01),
        'lru_w_i': normal(keys[8], (n_even, LRU_HEADS, LRU_BLOCK_W, LRU_BLOCK_W), LRU_BLOCK_W ** -0.5),
        'lru_b_i': normal(keys[9], (n_even, LRU_HEADS, LRU_BLOCK_W), 0.01),
        'lru_lambda': lam,
        'q_norm': gain(keys[11], (n_even, ATT_HEAD_DIM)),
        'k_norm': gain(keys[12], (n_even, ATT_HEAD_DIM)),
        'attn_sinks': normal(keys[13], (n_even, ATT_HEADS), 0.5),
        'ab_w_out': normal(keys[14], (n_even, AB_OUT_WIDTH, D_MODEL), AB_OUT_WIDTH ** -0.5),
        'mix_norm_ret': gain(keys[15], (n_odd, D_MODEL)),
        'ret_w_in': normal(keys[16], (n_odd, D_MODEL, RET_IN_WIDTH), D_MODEL ** -0.5),
        'ret_w_out': normal(keys[17], (n_odd, 2 * D_MODEL, D_MODEL), (2 * D_MODEL) ** -0.5),
        'ffn_norm': gain(keys[18], (DEPTH, D_MODEL)),
        'ffn_w_gu': normal(keys[19], (DEPTH, D_MODEL, 2 * D_FF), D_MODEL ** -0.5),
        'ffn_w_down': normal(keys[20], (DEPTH, D_FF, D_MODEL), D_FF ** -0.5),
    }

def first_block(x, meta_tokens, mix_norm_ab, ab_w_in, lru_conv_w, lru_conv_b, lru_w_a, lru_b_a,
              lru_w_i, lru_b_i, lru_lambda, q_norm, k_norm, attn_sinks, ab_w_out,
              mix_norm_ret, ret_w_in, ret_w_out, ffn_norm, ffn_w_gu, ffn_w_down):
    B = x.shape[0]
    meta = jnp.broadcast_to(meta_tokens[None].astype(x.dtype), (B, N_META, D_MODEL))
    h = jnp.concatenate([meta, x], axis=1)
    T = h.shape[1]
    att_cos, att_sin = _rope_tables(T, ROT_DIM, ROPE_THETA)
    ret_cos, ret_sin = _rope_tables(T, RET_QK_DIM, RET_THETA)
    for layer in range(DEPTH):
        j = layer // 2
        if layer % 2 == 0:
            h = h + _mixer_rglru_swa(_rmsnorm(h, mix_norm_ab[j]), att_cos, att_sin, ab_w_in[j],
                                     lru_conv_w[j], lru_conv_b[j], lru_w_a[j], lru_b_a[j],
                                     lru_w_i[j], lru_b_i[j], lru_lambda[j], q_norm[j], k_norm[j],
                                     attn_sinks[j], ab_w_out[j])
        else:
            h = h + _mixer_retention(_rmsnorm(h, mix_norm_ret[j]), ret_cos, ret_sin,
                                     ret_w_in[j], ret_w_out[j])
        h = h + _swiglu(_rmsnorm(h, ffn_norm[layer]), ffn_w_gu[layer], ffn_w_down[layer])
    return h[:, N_META:]


N_MIXERS = 2
N_A_LAYERS = (DEPTH + 1) // 2
N_B_LAYERS = DEPTH // 2

GDN_HEADS = 8
GDN_DK = 128
GDN_DV = 128
GDN_CONV = 4
GDN_CHUNK = 64
GDN_HK = GDN_HEADS * GDN_DK
GDN_HV = GDN_HEADS * GDN_DV
GDN_IN = 2 * GDN_HK + 2 * GDN_HV + 2 * GDN_HEADS
GDN_CONV_CH = 2 * GDN_HK + GDN_HV

DSW_GROUPS = ((128, 1), (512, 4), (2048, 16))
DSW_N_GROUPS = len(DSW_GROUPS)
DSW_HEADS = 8
DSW_DH = 64
DSW_HG = DSW_HEADS * DSW_DH
DSW_IN = 3 * DSW_N_GROUPS * DSW_HG

REL_BUCKETS = 32
REL_MAX_DIST = 2048
REL_HEADS = DSW_N_GROUPS * DSW_HEADS

FFN_HIDDEN = -(-8 * D_MODEL // (3 * 256)) * 256


def rms_norm(x, gain):
    xf = x.astype(jnp.float32)
    y = xf * lax.rsqrt(jnp.mean(xf * xf, axis=-1, keepdims=True) + RMS_EPS)
    return y * gain.astype(jnp.float32)

def l2_norm(x):
    xf = x.astype(jnp.float32)
    return xf * lax.rsqrt(jnp.sum(xf * xf, axis=-1, keepdims=True) + RMS_EPS)

def causal_depthwise_conv(x, w):
    K, C = w.shape
    return lax.conv_general_dilated(
        x, w[:, None, :].astype(x.dtype), window_strides=(1,),
        padding=((K - 1, 0),), dimension_numbers=("NWC", "WIO", "NWC"),
        feature_group_count=C)

def chunk_gated_delta_rule(q, k, v, g, beta):
    Bsz, S, H, dk = q.shape
    dv = v.shape[-1]
    C = GDN_CHUNK
    N = S // C
    to_chunks = lambda t: jnp.transpose(t.reshape(Bsz, N, C, H, t.shape[-1]), (0, 3, 1, 2, 4))
    q = to_chunks(q * (dk ** -0.5))
    k = to_chunks(k)
    v = to_chunks(v.astype(jnp.float32))
    beta = jnp.transpose(beta.reshape(Bsz, N, C, H), (0, 3, 1, 2))
    g = jnp.cumsum(jnp.transpose(g.reshape(Bsz, N, C, H), (0, 3, 1, 2)), axis=-1)

    causal = jnp.tril(jnp.ones((C, C), dtype=bool))
    strict = jnp.tril(jnp.ones((C, C), dtype=bool), -1)
    decay = jnp.exp(jnp.where(causal, g[..., :, None] - g[..., None, :], -jnp.inf))
    kb = k * beta[..., None]
    vb = v * beta[..., None]
    Lmat = jnp.where(strict, jnp.einsum('bhncd,bhnmd->bhncm', kb, k) * decay, 0.0)
    rhs = jnp.concatenate([vb, kb * jnp.exp(g)[..., None]], axis=-1)
    sol = lax.linalg.triangular_solve(Lmat, rhs, left_side=True, lower=True, unit_diagonal=True)
    u = sol[..., :dv]
    w = sol[..., dv:]
    qk = jnp.where(causal, jnp.einsum('bhncd,bhnmd->bhncm', q, k) * decay, 0.0)

    g_last = g[..., -1]
    q_dec = q * jnp.exp(g)[..., None]
    k_dec = k * jnp.exp(g_last[..., None] - g)[..., None]

    def step(state, inp):
        qd, a, uu, ww, kd, gl = inp
        v_new = uu - jnp.einsum('bhck,bhkv->bhcv', ww, state)
        o = jnp.einsum('bhck,bhkv->bhcv', qd, state) + jnp.einsum('bhcm,bhmv->bhcv', a, v_new)
        state = state * jnp.exp(gl)[..., None, None] + jnp.einsum('bhck,bhcv->bhkv', kd, v_new)
        return state, o

    xs = tuple(jnp.moveaxis(t, 2, 0) for t in (q_dec, qk, u, w, k_dec, g_last))
    state0 = jnp.zeros((Bsz, H, dk, dv), jnp.float32)
    _, o = lax.scan(step, state0, xs)
    return jnp.transpose(o, (1, 0, 3, 2, 4)).reshape(Bsz, S, H, dv)

def gated_deltanet_mixer(h, w_in, conv_w, a_log, dt_bias, out_gain, w_out):
    Bsz, S, _ = h.shape
    proj = h @ w_in
    qkv, z, a, b = jnp.split(proj, [GDN_CONV_CH, GDN_CONV_CH + GDN_HV,
                                    GDN_CONV_CH + GDN_HV + GDN_HEADS], axis=-1)
    qkv = jax.nn.silu(causal_depthwise_conv(qkv, conv_w))
    q, k, v = jnp.split(qkv, [GDN_HK, 2 * GDN_HK], axis=-1)
    q = l2_norm(q.reshape(Bsz, S, GDN_HEADS, GDN_DK))
    k = l2_norm(k.reshape(Bsz, S, GDN_HEADS, GDN_DK))
    v = v.reshape(Bsz, S, GDN_HEADS, GDN_DV)
    beta = jax.nn.sigmoid(b.astype(jnp.float32))
    g = -jnp.exp(a_log.astype(jnp.float32)) * jax.nn.softplus(a.astype(jnp.float32) + dt_bias.astype(jnp.float32))
    o = chunk_gated_delta_rule(q, k, v, g, beta)
    zf = z.reshape(Bsz, S, GDN_HEADS, GDN_DV).astype(jnp.float32)
    o = rms_norm(o, out_gain) * jax.nn.silu(zf)
    return o.reshape(Bsz, S, GDN_HV).astype(h.dtype) @ w_out

def t5_causal_bucket(dist):
    max_exact = REL_BUCKETS // 2
    scaled = jnp.log(jnp.maximum(dist, 1).astype(jnp.float32) / max_exact) / math.log(REL_MAX_DIST / max_exact)
    large = max_exact + (scaled * (REL_BUCKETS - max_exact)).astype(jnp.int32)
    large = jnp.minimum(large, REL_BUCKETS - 1)
    return jnp.where(dist < max_exact, dist, large)

def dilated_window_group(q, k, v, bias_table, window, dilation):
    Bsz, S, H, dh = q.shape
    span = window // dilation
    blk = span
    unit = dilation * blk
    S_pad = -(-S // unit) * unit
    nb = S_pad // unit

    def sub(t):
        t = jnp.pad(t, ((0, 0), (0, S_pad - S), (0, 0), (0, 0)))
        return jnp.transpose(t.reshape(Bsz, nb, blk, dilation, H, dh), (0, 3, 1, 2, 4, 5))

    qs, ks, vs = sub(q), sub(k), sub(v)
    shift = lambda t: jnp.concatenate([jnp.zeros_like(t[:, :, :1]), t[:, :, :-1]], axis=2)
    kb = jnp.concatenate([shift(ks), ks], axis=3)
    vb = jnp.concatenate([shift(vs), vs], axis=3)

    qi = jnp.arange(blk)[:, None] + blk
    ki = jnp.arange(2 * blk)[None, :]
    dist = qi - ki
    band = (dist >= 0) & (dist <= span)
    valid = band[None] & ((jnp.arange(nb) > 0)[:, None, None] | (ki >= blk)[None])
    bias = jnp.transpose(bias_table.astype(jnp.float32)[t5_causal_bucket(jnp.maximum(dist, 0) * dilation)], (2, 0, 1))

    logits = jnp.einsum('brnqhd,brnkhd->brnhqk', qs, kb) + bias[None, None, None]
    logits = jnp.where(valid[None, None, :, None], logits, -jnp.inf)
    m = jnp.max(logits, axis=-1, keepdims=True)
    p = jnp.exp(logits - m)
    l = jnp.sum(p, axis=-1, keepdims=True)
    o = jnp.einsum('brnhqk,brnkhd->brnqhd', p / l, vb)
    lse = (m + jnp.log(l))[..., 0]
    o = jnp.transpose(o, (0, 2, 3, 1, 4, 5)).reshape(Bsz, S_pad, H, dh)[:, :S]
    lse = jnp.transpose(lse, (0, 2, 4, 1, 3)).reshape(Bsz, S_pad, H)[:, :S]
    return o, lse

def dilated_attention_mixer(h, w_in, q_gain, k_gain, rel_bias, w_out):
    Bsz, S, _ = h.shape
    proj = (h @ w_in).reshape(Bsz, S, 3, DSW_N_GROUPS, DSW_HEADS, DSW_DH)
    q = rms_norm(proj[:, :, 0], q_gain) * (DSW_DH ** -0.5)
    k = rms_norm(proj[:, :, 1], k_gain)
    v = proj[:, :, 2].astype(jnp.float32)
    outs, lses = [], []
    for gi, (window, dilation) in enumerate(DSW_GROUPS):
        o, lse = dilated_window_group(q[:, :, gi], k[:, :, gi], v[:, :, gi],
                                      rel_bias[:, gi * DSW_HEADS:(gi + 1) * DSW_HEADS], window, dilation)
        outs.append(o)
        lses.append(lse)
    wts = jax.nn.softmax(jnp.stack(lses), axis=0)
    o = jnp.sum(wts[..., None] * jnp.stack(outs), axis=0)
    return o.reshape(Bsz, S, DSW_HG).astype(h.dtype) @ w_out

def swiglu(h, w_in, w_out):
    gate, up = jnp.split(h @ w_in, 2, axis=-1)
    return (jax.nn.silu(gate) * up) @ w_out

def second_inputs(seed: int = 0) -> dict:
    key = jax.random.key(seed)
    ks = jax.random.split(key, 20)
    nrm = lambda k, shape, s: jax.random.normal(k, shape, jnp.float32) * s
    D = D_MODEL
    a_init = jax.random.uniform(ks[10], (N_A_LAYERS, GDN_HEADS), jnp.float32, 1.0, 16.0)
    dt = jnp.exp(jax.random.uniform(ks[11], (N_A_LAYERS, GDN_HEADS), jnp.float32,
                                    math.log(1e-3), math.log(1e-1)))
    return {
        "x": nrm(ks[0], (BATCH, SEQ, D), 1.0),
        "c": nrm(ks[1], (BATCH, D), 1.0),
        "w_ada": nrm(ks[2], (DEPTH, D, 6 * D), D ** -0.5),
        "b_ada": nrm(ks[3], (DEPTH, 6 * D), 0.02),
        "norm_mix": 1.0 + nrm(ks[4], (DEPTH, D), 0.02),
        "norm_ffn": 1.0 + nrm(ks[5], (DEPTH, D), 0.02),
        "w_ffn_in": nrm(ks[6], (DEPTH, D, 2 * FFN_HIDDEN), D ** -0.5),
        "w_ffn_out": nrm(ks[7], (DEPTH, FFN_HIDDEN, D), FFN_HIDDEN ** -0.5),
        "gdn_w_in": nrm(ks[8], (N_A_LAYERS, D, GDN_IN), D ** -0.5),
        "gdn_conv": nrm(ks[9], (N_A_LAYERS, GDN_CONV, GDN_CONV_CH), GDN_CONV ** -0.5),
        "gdn_a_log": jnp.log(a_init),
        "gdn_dt_bias": dt + jnp.log(-jnp.expm1(-dt)),
        "gdn_out_norm": 1.0 + nrm(ks[12], (N_A_LAYERS, GDN_DV), 0.02),
        "gdn_w_out": nrm(ks[13], (N_A_LAYERS, GDN_HV, D), GDN_HV ** -0.5),
        "dsw_w_in": nrm(ks[14], (N_B_LAYERS, D, DSW_IN), D ** -0.5),
        "dsw_q_norm": 1.0 + nrm(ks[15], (N_B_LAYERS, DSW_DH), 0.02),
        "dsw_k_norm": 1.0 + nrm(ks[16], (N_B_LAYERS, DSW_DH), 0.02),
        "dsw_w_out": nrm(ks[17], (N_B_LAYERS, DSW_HG, D), DSW_HG ** -0.5),
        "rel_bias": nrm(ks[18], (REL_BUCKETS, REL_HEADS), 0.5),
    }

def second_block(x, c, w_ada, b_ada, norm_mix, norm_ffn, w_ffn_in, w_ffn_out,
              gdn_w_in, gdn_conv, gdn_a_log, gdn_dt_bias, gdn_out_norm, gdn_w_out,
              dsw_w_in, dsw_q_norm, dsw_k_norm, dsw_w_out, rel_bias):
    cond = jax.nn.silu(c.astype(jnp.float32))
    for layer in range(DEPTH):
        mod = (cond @ w_ada[layer].astype(jnp.float32) + b_ada[layer].astype(jnp.float32)).astype(x.dtype)
        sh1, sc1, g1, sh2, sc2, g2 = jnp.split(mod[:, None, :], 6, axis=-1)

        h = (rms_norm(x, norm_mix[layer]) * (1.0 + sc1) + sh1).astype(x.dtype)
        j = layer // N_MIXERS
        if layer % N_MIXERS == 0:
            y = gated_deltanet_mixer(h, gdn_w_in[j], gdn_conv[j], gdn_a_log[j], gdn_dt_bias[j],
                                     gdn_out_norm[j], gdn_w_out[j])
        else:
            y = dilated_attention_mixer(h, dsw_w_in[j], dsw_q_norm[j], dsw_k_norm[j],
                                        rel_bias, dsw_w_out[j])
        x = x + g1 * y

        h = (rms_norm(x, norm_ffn[layer]) * (1.0 + sc2) + sh2).astype(x.dtype)
        x = x + g2 * swiglu(h, w_ffn_in[layer], w_ffn_out[layer])
    return x


def setup_inputs(seed=0):
    out = dict(first_inputs(seed))
    for name, value in second_inputs(seed + 1).items():
        if name != "x":
            out[name + "_2"] = value
    return out


def reference(
    x, meta_tokens, mix_norm_ab, ab_w_in, lru_conv_w, lru_conv_b, lru_w_a, lru_b_a, lru_w_i,
    lru_b_i, lru_lambda, q_norm, k_norm, attn_sinks, ab_w_out, mix_norm_ret, ret_w_in,
    ret_w_out, ffn_norm, ffn_w_gu, ffn_w_down, c_2, w_ada_2, b_ada_2, norm_mix_2, norm_ffn_2,
    w_ffn_in_2, w_ffn_out_2, gdn_w_in_2, gdn_conv_2, gdn_a_log_2, gdn_dt_bias_2, gdn_out_norm_2,
    gdn_w_out_2, dsw_w_in_2, dsw_q_norm_2, dsw_k_norm_2, dsw_w_out_2, rel_bias_2,
):
    x = first_block(
        x, meta_tokens, mix_norm_ab, ab_w_in, lru_conv_w, lru_conv_b, lru_w_a, lru_b_a, lru_w_i,
        lru_b_i, lru_lambda, q_norm, k_norm, attn_sinks, ab_w_out, mix_norm_ret, ret_w_in,
        ret_w_out, ffn_norm, ffn_w_gu, ffn_w_down,
    )
    return second_block(
        x, c_2, w_ada_2, b_ada_2, norm_mix_2, norm_ffn_2, w_ffn_in_2, w_ffn_out_2, gdn_w_in_2,
        gdn_conv_2, gdn_a_log_2, gdn_dt_bias_2, gdn_out_norm_2, gdn_w_out_2, dsw_w_in_2,
        dsw_q_norm_2, dsw_k_norm_2, dsw_w_out_2, rel_bias_2,
    )


_drawn_inputs = setup_inputs


def setup_inputs(seed=0):
    import zlib

    import numpy as np

    out = dict(_drawn_inputs(seed))
    spreads = {}
    factors = {'mix_norm_ab': 3.649,
     'lru_b_a': 8.0,
     'lru_b_i': 8.0,
     'q_norm': 8.0,
     'k_norm': 8.0,
     'attn_sinks': 64.0,
     'norm_mix_2': 5.546,
     'norm_ffn_2': 4.189,
     'gdn_out_norm_2': 7.702,
     'dsw_q_norm_2': 23.528,
     'dsw_k_norm_2': 8.0,
     'mix_norm_ret': 3.031,
     'ffn_norm': 3.259,
     'rel_bias_2': 5.294}
    for name, (base, spread) in spreads.items():
        noise = np.random.default_rng([zlib.crc32(name.encode()), seed]).standard_normal(out[name].shape)
        drawn = base * np.exp(spread * noise) if base else spread * noise
        out[name] = __import__('jax').numpy.asarray(drawn.astype(out[name].dtype))
    for name, factor in factors.items():
        out[name] = (out[name] * factor).astype(out[name].dtype)
    return out
```

```python
from contextlib import ExitStack
import math

import numpy as np
import concourse.bass as bass
from concourse import mybir

ALU = mybir.AluOpType
ACT = mybir.ActivationFunctionType
AX_X = mybir.AxisListType.X
F32 = mybir.dt.float32
F32R = mybir.dt.float32r

P = 128
D = 1024
DC = D // P
SEQ = 512
N_META = 16
T = SEQ + N_META
BLOCK = 128
QB = SEQ // BLOCK
EPS = 1e-6
MASKED = -1e30

LRU_W = 512
LRU_CH = LRU_W // P
LRU_C = 8.0
HD = 64
ATT_HEADS = 8
ATT_CH = ATT_HEADS * HD // P
RET_HEADS = 4
RET_V = 512
D_FF = 2816
FF_CH = D_FF // P
GDN_HEADS = 8
GDN_CH = 3 * GDN_HEADS
DSW_HEADS = 8
DSW_GROUPS = ((128, 1), (512, 4), (2048, 16))
REL_BUCKETS = 32
REL_MAX = 2048

SLOT = 2048
ALL = (0, 2)
ONLY_X = (N_META, 1)


def width(cols):
    return (T - cols[0]) // cols[1]


class Chain:

    def __init__(self, sem):
        self.sem, self.n = sem, 0

    def link(self, eng, ins):
        self.n += 1
        ins.then_inc(self.sem, 1)
        eng.wait_ge(self.sem, self.n)


class Weights:

    def __init__(self, name, tiles, unroll, shape, source, split=True):
        self.name, self.tiles, self.unroll = name, tiles, unroll
        self.rows, self.cols = shape
        self.size = self.rows * self.cols
        self.source, self.split = source, split
        self.trips = tiles // unroll
        assert self.trips * unroll == tiles and (self.trips == 1 or unroll % 2 == 0)
        assert self.size <= SLOT


class Core:

    def __init__(self, nc, ctx):
        self.nc, self.ctx = nc, ctx
        self.layer_sems = []
        self.x = self.sb("x_stream", [P, DC, T])
        self.raw = self.sb("w_raw", [P, 2, SLOT])
        self.w_hi = self.sb("w_hi", [P, 2, SLOT], F32R)
        self.w_lo = self.sb("w_lo", [P, 2, SLOT], F32R)
        self.ps = ctx.enter_context(nc.psum_tensor("ps", [P, 8, 512], F32))
        self.tile_loaded = [self.sem("tile_loaded_0"), self.sem("tile_loaded_1")]
        self.hi_ready = self.sem("hi_ready")
        self.lo_ready = self.sem("lo_ready")
        self.tile_used = self.sem("tile_used")
        self.psum_free = self.sem("psum_free")
        self.norm = {n: [self.sem("norm_" + n), 0] for n in
                     ("squares", "sum", "total", "var", "std", "scaled", "hi")}
        self.up = {n: [self.sem("up_" + n), 0] for n in ("silu", "product", "hi", "lo")}
        self.up["product"][1] = self.up["lo"][1] = 2
        self.dve = Chain(self.sem("dve_chain"))
        self.act = Chain(self.sem("act_chain"))
        self.pool = Chain(self.sem("pool_chain"))
        self.outs_freed = 2
        self.core_sems, self.layer_sems = self.layer_sems, []

    def sb(self, name, shape, dt=F32, ctx=None):
        return (ctx or self.ctx).enter_context(self.nc.sbuf_tensor(name, shape, dt))

    def take_h(self, name, ctx, chunks=DC):
        self.h_hi = self.sb(name + "_hi", [P, chunks, T], F32R, ctx)
        self.h_lo = self.sb(name + "_lo", [P, chunks, T], F32R, ctx)

    def sem(self, name):
        handle = self.nc.alloc_semaphore(name=name)
        self.layer_sems.append(handle)
        return handle

    def end_layer(self):
        self.nc.clear_and_free_semaphores(self.layer_sems)
        self.nc.all_engine_barrier()
        self.layer_sems = []

    def plan(self, weights):
        tile, incs = 2, [0, 0]
        for n, w in enumerate(weights):
            w.first, w.incs = tile, list(incs)
            w.next = weights[n + 1] if n + 1 < len(weights) else None
            for j in range(w.tiles):
                incs[(tile + j) % 2] += 16 * w.loads
            tile += w.tiles

    def slot(self, w, j):
        return (w.first + j) % 2

    def tile_no(self, w, i, j):
        return w.first + j + w.unroll * i

    def after(self, w, i, j, ahead, last):
        j += ahead
        if j < w.unroll:
            return w, i, j
        if not last:
            return w, i + 1, j - w.unroll
        j -= w.unroll
        n = w.next
        while n and j >= n.tiles:
            j -= n.tiles
            n = n.next
        return (n, 0, j) if n else None

    def load(self, eng, w, i, j):
        s = self.slot(w, j)
        for dst, src in w.source(i, j):
            eng.dma_start(dst(self.raw[:, s, 0:w.size]), src).then_inc(self.tile_loaded[s], 16)

    def loads(self, sp, w, i, last):
        for j in range(w.unroll):
            sp.wait_ge(self.lo_ready, self.tile_no(w, i, j) + 1)
            ahead = self.after(w, i, j, 2, last)
            if ahead:
                self.load(sp, *ahead)

    def wait_loaded(self, eng, w, i, j):
        s = self.slot(w, j)
        n = 16 * w.loads * (j // 2 + 1)
        eng.wait_ge(self.tile_loaded[s], i * (16 * w.loads * (w.unroll // 2)) + (w.incs[s] + n))

    def split_hi(self, act, w, i, j):
        s = self.slot(w, j)
        self.wait_loaded(act, w, i, j)
        act.wait_ge(self.tile_used, self.tile_no(w, i, j) - 1)
        self.nc.scalar.activation(self.w_hi[:, s, 0:w.size], self.raw[:, s, 0:w.size],
                                  ACT.Copy).then_inc(self.hi_ready, 1)

    def split_lo(self, dve, w, i, j):
        s = self.slot(w, j)
        dve.wait_ge(self.hi_ready, self.tile_no(w, i, j) + 1)
        self.nc.vector.tensor_tensor(self.w_lo[:, s, 0:w.size], self.raw[:, s, 0:w.size],
                                     self.w_hi[:, s, 0:w.size].bitcast(F32),
                                     ALU.subtract).then_inc(self.lo_ready, 1)

    def split_ahead(self, half, eng, w, i, j, last):
        ahead = self.after(w, i, j, 1, last)
        if ahead:
            half(eng, *ahead)

    def weights(self, w, j, half):
        return half[:, self.slot(w, j), 0:w.size].rearrange("p (k c) -> p k c", k=w.rows)

    def over_tiles(self, eng, w, trip):
        if w.trips > 2:
            with eng.Fori(0, w.trips - 1) as i:
                trip(i, False)
        else:
            for i in range(w.trips - 1):
                trip(i, False)
        trip(w.trips - 1, True)

    def out_psum(self, q, cols):
        n = cols[1]
        return self.ps[:, q * n:(q + 1) * n, 0:width(cols)]

    def spans(self, ap, cols):
        return ap.rearrange("p (s w) -> p s w", s=cols[1])

    def chunk(self, buf, o, cols, base=0):
        c = buf[:, bass.ds(o, 1), cols[0] - base:T - base]
        return c.rearrange("p o (s w) -> p (o s) w", s=cols[1])


def split_products(nc, out, w_hi, w_lo, h_hi, h_lo, first, last):
    nc.tensor.matmul(out, w_hi, h_hi, start=first, stop=False)
    nc.tensor.matmul(out, w_hi, h_lo, start=False, stop=False)
    return nc.tensor.matmul(out, w_lo, h_hi, start=False, stop=last)


def normalize(K, cols, gain, shift=None):
    nc = K.nc
    c0, ns = cols
    W = T - c0
    n = {k: v[1] for k, v in K.norm.items()}
    sems = {k: v[0] for k, v in K.norm.items()}
    with ExitStack() as ctx:
        sq = K.sb("squares_%d" % n["sum"], [P, DC, W], ctx=ctx)
        rstd = K.sb("rstd_%d" % n["sum"], [P, W], ctx=ctx)
        with nc.Block() as block:
            @block.scalar
            def _(act):
                for g in range(2):
                    nc.scalar.activation(sq[:, 4 * g:4 * g + 4, :], K.x[:, 4 * g:4 * g + 4, c0:T],
                                         ACT.Square).then_inc(sems["squares"], 1)
                act.wait_ge(sems["var"], n["var"] + 1)
                nc.scalar.activation(rstd[:], rstd[:], ACT.Sqrt).then_inc(sems["std"], 1)
                for c in range(DC):
                    act.wait_ge(sems["scaled"], n["scaled"] + c + 1)
                    if shift is None:
                        ins = nc.scalar.activation(K.h_hi[:, c, c0:T], sq[:, c, :], ACT.Copy)
                    else:
                        ins = nc.scalar.activation(K.h_hi[:, c, c0:T], sq[:, c, :], ACT.Identity,
                                                   bias=shift[:, c:c + 1])
                    ins.then_inc(sems["hi"], 1)

            @block.vector
            def _(dve):
                dve.wait_ge(sems["squares"], n["squares"] + 2)
                K.dve.link(dve, nc.vector.tensor_tensor(sq[:, 0:4, :], sq[:, 0:4, :], sq[:, 4:8, :], ALU.add))
                K.dve.link(dve, nc.vector.tensor_tensor(sq[:, 0:2, :], sq[:, 0:2, :], sq[:, 2:4, :], ALU.add))
                nc.vector.tensor_tensor(sq[:, 0, :], sq[:, 0, :], sq[:, 1, :], ALU.add)\
                    .then_inc(sems["sum"], 1)
                dve.wait_ge(sems["total"], n["total"] + 1)
                nc.vector.tensor_scalar(K.spans(rstd[:], cols), K.out_psum(0, cols), 1.0 / D, EPS,
                                        ALU.mult, ALU.add).then_inc(sems["var"], 1)
                dve.wait_ge(sems["std"], n["std"] + 1)
                K.dve.link(dve, nc.vector.reciprocal(rstd[:], rstd[:]))
                def scale(c):
                    nc.vector.scalar_tensor_tensor(sq[:, c, :], K.x[:, c, c0:T], gain[:, c:c + 1], rstd[:],
                                                   ALU.mult, ALU.mult).then_inc(sems["scaled"], 1)
                def rest(c):
                    dve.wait_ge(sems["hi"], n["hi"] + c + 1)
                    hi = K.h_hi[:, c, c0:T].bitcast(F32)
                    if shift is None:
                        nc.vector.tensor_tensor(K.h_lo[:, c, c0:T], sq[:, c, :], hi, ALU.subtract)
                    else:
                        nc.vector.scalar_tensor_tensor(K.h_lo[:, c, c0:T], sq[:, c, :], shift[:, c:c + 1], hi,
                                                       ALU.add, ALU.subtract)
                scale(0)
                for c in range(1, DC):
                    scale(c)
                    rest(c - 1)
                rest(DC - 1)

            @block.tensor
            def _(pe):
                pe.wait_ge(sems["sum"], n["sum"] + 1)
                w = width(cols)
                for s in range(ns):
                    mm = nc.tensor.matmul(K.ps[:, s, 0:w], K.ones[:], sq[:, 0, s * w:(s + 1) * w],
                                          start=True, stop=True)
                mm.then_inc(sems["total"], 1)
    for k, by in (("squares", 2), ("sum", 1), ("total", 1), ("var", 1), ("std", 1), ("scaled", DC), ("hi", DC)):
        K.norm[k][1] += by


def project(K, w, dest, cols, base=0):
    nc = K.nc
    wd = width(cols)
    M = w.cols // P
    freed = K.outs_freed
    with nc.Block() as block:
        @block.sync
        def _(sp):
            K.over_tiles(sp, w, lambda i, last: K.loads(sp, w, i, last))

        @block.scalar
        def _(act):
            def trip(i, last):
                for j in range(w.unroll):
                    K.split_ahead(K.split_hi, act, w, i, j, last)
                    act.wait_ge(K.tile_used, K.tile_no(w, i, j) + 1)
                    for m in range(M):
                        ins = nc.scalar.activation(K.chunk(dest, (w.unroll * i + j) * M + m, cols, base),
                                                   K.out_psum((j % 2) * M + m, cols), ACT.Copy)
                    ins.then_inc(K.psum_free, 1)
            K.over_tiles(act, w, trip)

        @block.vector
        def _(dve):
            def trip(i, last):
                for j in range(w.unroll):
                    K.split_ahead(K.split_lo, dve, w, i, j, last)
            K.over_tiles(dve, w, trip)

        @block.tensor
        def _(pe):
            def trip(i, last):
                for j in range(w.unroll):
                    pe.wait_ge(K.lo_ready, K.tile_no(w, i, j) + 1)
                    pe.wait_ge(K.psum_free, i * w.unroll + (freed + j - 1))
                    hi, lo = K.weights(w, j, K.w_hi), K.weights(w, j, K.w_lo)
                    for m in range(M):
                        for s in range(cols[1]):
                            at = slice(cols[0] + s * wd, cols[0] + (s + 1) * wd)
                            for k in range(w.rows):
                                mm = split_products(
                                    nc, K.ps[:, ((j % 2) * M + m) * cols[1] + s, 0:wd],
                                    hi[:, k, m * P:(m + 1) * P], lo[:, k, m * P:(m + 1) * P],
                                    K.h_hi[:, k, at], K.h_lo[:, k, at], k == 0, k == w.rows - 1)
                    mm.then_inc(K.tile_used, 1)
            K.over_tiles(pe, w, trip)
    K.outs_freed += w.tiles


def project_tokens(K, w, blocks, dest):
    nc = K.nc
    freed = K.outs_freed

    def place(j, b, rows):
        return K.ps[0:rows, (j % 2) * 4 + b // 2, (b % 2) * 256:(b % 2) * 256 + w.cols]
    with nc.Block() as block:
        @block.sync
        def _(sp):
            K.over_tiles(sp, w, lambda i, last: K.loads(sp, w, i, last))

        @block.scalar
        def _(act):
            def trip(i, last):
                for j in range(w.unroll):
                    K.split_ahead(K.split_hi, act, w, i, j, last)
                    act.wait_ge(K.tile_used, K.tile_no(w, i, j) + 1)
                    for b, (view, rows) in enumerate(blocks):
                        ins = nc.scalar.activation(dest(b, i, j), place(j, b, rows), ACT.Copy)
                    ins.then_inc(K.psum_free, 1)
            K.over_tiles(act, w, trip)

        @block.vector
        def _(dve):
            def trip(i, last):
                for j in range(w.unroll):
                    K.split_ahead(K.split_lo, dve, w, i, j, last)
            K.over_tiles(dve, w, trip)

        @block.tensor
        def _(pe):
            def trip(i, last):
                for j in range(w.unroll):
                    pe.wait_ge(K.lo_ready, K.tile_no(w, i, j) + 1)
                    pe.wait_ge(K.psum_free, i * w.unroll + (freed + j - 1))
                    hi, lo = K.weights(w, j, K.w_hi), K.weights(w, j, K.w_lo)
                    for b, (view, rows) in enumerate(blocks):
                        for k in range(w.rows):
                            mm = split_products(nc, place(j, b, P), view(K.h_hi, k), view(K.h_lo, k),
                                                hi[:, k, :], lo[:, k, :], k == 0, k == w.rows - 1)
                    mm.then_inc(K.tile_used, 1)
            K.over_tiles(pe, w, trip)
    K.outs_freed += w.tiles


def add_projected(K, w, src, cols, parts=1, base=0, gate=None):
    nc = K.nc
    wd = width(cols)
    M = w.cols // P
    freed = K.outs_freed
    per = w.unroll // parts
    with nc.Block() as block:
        @block.sync
        def _(sp):
            K.over_tiles(sp, w, lambda i, last: K.loads(sp, w, i, last))

        @block.scalar
        def _(act):
            def trip(i, last):
                for j in range(w.unroll):
                    K.split_ahead(K.split_hi, act, w, i, j, last)
            K.over_tiles(act, w, trip)

        @block.vector
        def _(dve):
            def trip(i, last):
                for j in range(w.unroll):
                    K.split_ahead(K.split_lo, dve, w, i, j, last)
                    if j % parts < parts - 1:
                        continue
                    g = j // parts
                    dve.wait_ge(K.tile_used, K.tile_no(w, i, j) + 1)
                    for m in range(M):
                        o = (per * i + g) * M + m
                        x = K.chunk(K.x, o, cols)
                        by = 1.0 if gate is None else gate[:, bass.ds(o, 1)]
                        ins = nc.vector.scalar_tensor_tensor(x, K.out_psum((g % 2) * M + m, cols), by, x,
                                                             ALU.mult, ALU.add)
                    ins.then_inc(K.psum_free, 1)
            K.over_tiles(dve, w, trip)

        @block.tensor
        def _(pe):
            def trip(i, last):
                for j in range(w.unroll):
                    g, part = j // parts, j % parts
                    pe.wait_ge(K.lo_ready, K.tile_no(w, i, j) + 1)
                    if part == 0:
                        pe.wait_ge(K.psum_free, i * per + (freed + g - 1))
                    hi, lo = K.weights(w, j, K.w_hi), K.weights(w, j, K.w_lo)
                    for m in range(M):
                        for s in range(cols[1]):
                            c0 = cols[0] - base + s * wd
                            for k in range(w.rows):
                                row = part * w.rows + k
                                mm = split_products(
                                    nc, K.ps[:, ((g % 2) * M + m) * cols[1] + s, 0:wd],
                                    hi[:, k, m * P:(m + 1) * P], lo[:, k, m * P:(m + 1) * P],
                                    src[0][:, row, c0:c0 + wd], src[1][:, row, c0:c0 + wd],
                                    row == 0, row == parts * w.rows - 1)
                    mm.then_inc(K.tile_used, 1)
            K.over_tiles(pe, w, trip)
    K.outs_freed += w.tiles // parts


def feed_forward(K, up, down, cols, gate=None):
    nc = K.nc
    wd = width(cols)
    W = T - cols[0]
    freed = K.outs_freed
    n = {k: v[1] for k, v in K.up.items()}
    sems = {k: v[0] for k, v in K.up.items()}
    with ExitStack() as ctx:
        a_hi = K.sb(up.name + "_act_hi", [P, FF_CH, W], F32R, ctx)
        a_lo = K.sb(up.name + "_act_lo", [P, FF_CH, W], F32R, ctx)
        silu = K.sb(up.name + "_silu", [P, W], ctx=ctx)
        prod = K.sb(up.name + "_prod", [P, 2, W], ctx=ctx)
        with nc.Block() as block:
            @block.sync
            def _(sp):
                K.over_tiles(sp, up, lambda i, last: K.loads(sp, up, i, last))

            @block.scalar
            def _(act):
                def trip(i, last):
                    for j in range(up.unroll):
                        o = i * up.unroll + j
                        K.split_ahead(K.split_hi, act, up, i, j, last)
                        act.wait_ge(K.tile_used, K.tile_no(up, i, j) + 1)
                        nc.scalar.activation(K.spans(silu[:], cols), K.out_psum((j % 2) * 2, cols),
                                             ACT.Silu).then_inc(sems["silu"], 1)
                        act.wait_ge(sems["product"], i * up.unroll + (n["product"] + j + 1))
                        nc.scalar.activation(a_hi[:, bass.ds(o, 1), :], prod[:, j % 2:j % 2 + 1, :],
                                             ACT.Copy).then_inc(sems["hi"], 1)
                K.over_tiles(act, up, trip)

            @block.vector
            def _(dve):
                def trip(i, last):
                    for j in range(up.unroll):
                        o = i * up.unroll + j
                        K.split_ahead(K.split_lo, dve, up, i, j, last)
                        dve.wait_ge(sems["silu"], i * up.unroll + (n["silu"] + j + 1))
                        dve.wait_ge(sems["lo"], i * up.unroll + (n["lo"] + j - 1))
                        nc.vector.tensor_tensor(K.spans(prod[:, j % 2, :], cols), K.spans(silu[:], cols),
                                                K.out_psum((j % 2) * 2 + 1, cols), ALU.mult)\
                            .then_inc(sems["product"], 1)
                        dve.wait_ge(sems["hi"], i * up.unroll + (n["hi"] + j + 1))
                        nc.vector.tensor_tensor(a_lo[:, bass.ds(o, 1), :], prod[:, j % 2:j % 2 + 1, :],
                                                a_hi[:, bass.ds(o, 1), :].bitcast(F32), ALU.subtract)\
                            .then_inc(sems["lo"], 1)
                K.over_tiles(dve, up, trip)

            @block.tensor
            def _(pe):
                def trip(i, last):
                    for j in range(up.unroll):
                        pe.wait_ge(K.lo_ready, K.tile_no(up, i, j) + 1)
                        pe.wait_ge(sems["product"], i * up.unroll + (n["product"] + j - 1))
                        hi, lo = K.weights(up, j, K.w_hi), K.weights(up, j, K.w_lo)
                        for m in range(2):
                            for s in range(cols[1]):
                                at = slice(cols[0] + s * wd, cols[0] + (s + 1) * wd)
                                for k in range(DC):
                                    mm = split_products(
                                        nc, K.ps[:, ((j % 2) * 2 + m) * cols[1] + s, 0:wd],
                                        hi[:, k, m * P:(m + 1) * P], lo[:, k, m * P:(m + 1) * P],
                                        K.h_hi[:, k, at], K.h_lo[:, k, at], k == 0, k == DC - 1)
                        mm.then_inc(K.tile_used, 1)
                K.over_tiles(pe, up, trip)
        for k in K.up:
            K.up[k][1] += up.tiles
        add_projected(K, down, (a_hi, a_lo), cols, parts=2, base=cols[0], gate=gate)


def column_weights(name, matrix, tiles, unroll, cols=256, first=0, split=True):
    rows = matrix.shape[0] // P
    rowwise = matrix.rearrange("(k p) c -> p k c", p=P)

    def source(i, j):
        at = first + j * cols + i * (unroll * cols)
        return [(lambda slot: slot.rearrange("p (k c) -> p k c", k=rows), rowwise[:, :, bass.ds(at, cols)])]
    w = Weights(name, tiles, unroll, (rows, cols), source, split)
    w.loads = 1
    return w


def up_weights(name, matrix):
    rowwise = matrix.rearrange("(k p) c -> p k c", p=P)

    def source(i, j):
        def part(g):
            return lambda slot: slot.rearrange("p (k g c) -> p k g c", k=DC, g=2)[:, :, g, :]
        return [(part(g), rowwise[:, :, bass.ds(i * (2 * P) + (j * P + g * D_FF), P)]) for g in range(2)]
    w = Weights(name, FF_CH, 2, (DC, 2 * P), source)
    w.loads = 2
    return w


def down_weights(name, matrix):
    rows = FF_CH // 2
    halves = matrix.rearrange("(h k p) c -> h p k c", p=P, h=2)

    def source(i, j):
        return [(lambda slot: slot.rearrange("p (k c) -> p k c", k=rows),
                 halves[j % 2][:, :, bass.ds(i * (2 * P) + (j // 2) * P, P)])]
    w = Weights(name, 2 * DC, 4, (rows, P), source)
    w.loads = 1
    return w


def rope_tables(half, theta):
    inv = np.power(np.float32(theta), -np.arange(half, dtype=np.float32) / np.float32(half)).astype(np.float32)
    ang = (np.arange(T, dtype=np.float32)[None, :] * inv[:, None]).astype(np.float32)
    return np.cos(ang).astype(np.float32), np.sin(ang).astype(np.float32)


def bucket(distance):
    exact = REL_BUCKETS // 2
    if distance < exact:
        return distance
    scaled = np.log(np.float32(distance) / np.float32(exact)) / np.float32(math.log(REL_MAX / exact))
    return min(exact + int(scaled * np.float32(REL_BUCKETS - exact)), REL_BUCKETS - 1)


def constants():
    f = np.float32
    i = np.arange(P)
    c = {"ident": np.eye(P, dtype=f)}
    c["head_ones"] = (i[:, None] // HD == i[None, :] // HD).astype(f)
    half = HD // 8
    turn = np.zeros((P, P), f)
    cos, sin = np.ones((P, T), f), np.zeros((P, T), f)
    table_cos, table_sin = rope_tables(half, 500000.0)
    for h in range(P // HD):
        for d in range(half):
            turn[h * HD + half + d, h * HD + d] = -1.0
            turn[h * HD + d, h * HD + half + d] = 1.0
            for r in (d, d + half):
                cos[h * HD + r], sin[h * HD + r] = table_cos[d], table_sin[d]
    c["turn"], c["att_cos"], c["att_sin"] = turn, cos, sin
    q, k = i[:, None], i[None, :]
    own = np.where(k <= q, 0, MASKED).astype(f)
    before = np.where(k > q, 0, MASKED).astype(f)
    free = np.zeros((P, N_META), f)
    c["window_mask"] = np.concatenate([free, before, own], 1)
    c["first_mask"] = np.concatenate([free, own], 1)
    c["meta_mask"] = own[0:N_META, 0:N_META]
    c["ret_cos"], c["ret_sin"] = rope_tables(P, 10000.0)
    gamma = 1.0 - np.exp2(-5.0 - np.arange(RET_HEADS))
    away = np.arange(SEQ)[None, :] - i[:, None]
    decay = np.where(away >= 0, gamma[:, None, None] ** np.maximum(away, 0), 0.0)
    c["ret_decay"] = decay.transpose(1, 0, 2).reshape(P, -1).astype(f)
    away = np.arange(SEQ)[None, :] + N_META - np.arange(N_META)[:, None]
    c["ret_decay_meta"] = (gamma[:, None, None] ** away).transpose(1, 0, 2).reshape(N_META, -1).astype(f)
    n = 2 * GDN_HEADS
    select = np.zeros((n, 2, GDN_HEADS, P), f)
    for h in range(GDN_HEADS):
        select[h, 0, h] = select[GDN_HEADS + h, 1, h] = 1.0
    c["gdn_select"] = select.reshape(n, -1)
    c["gdn_causal"] = np.where(i[None, :] >= i[:, None], 0, MASKED).astype(f)
    j_, i_ = i[:, None], i[None, :]
    c["gdn_levels"] = np.stack([(i_ >> (n + 1) == j_ >> (n + 1)) & (i_ >> n & 1 == 1) & (j_ >> n & 1 == 0)
                                for n in range(7)], 1).reshape(P, -1).astype(f)
    picks = []
    for (window, dilation), (nk, first, step, every) in zip(DSW_GROUPS, bias_windows()):
        dist = first + P - 1 - np.arange(P + nk - 1)
        pick = np.zeros((REL_BUCKETS + 1, len(dist)), f)
        for m, away in enumerate(dist):
            ok = away % every == 0 and 0 <= away * step <= window
            pick[bucket(away * step) if ok else REL_BUCKETS, m] = 1.0 if ok else MASKED
        picks.append(pick)
    c["dsw_pick"] = np.concatenate(picks, 1)
    spread = np.zeros((DSW_HEADS, ATT_CH, P), f)
    for h in range(DSW_HEADS):
        spread[h, h // 2, (h % 2) * HD:(h % 2 + 1) * HD] = 1.0
    c["dsw_spread"] = spread.reshape(DSW_HEADS, -1)
    return {name: np.ascontiguousarray(v) for name, v in c.items()}


def load_all(K, block_name, pairs, sem):
    for dst, src in pairs:
        block_name.dma_start(dst, src).then_inc(sem, 16)


def prologue(K, I, first_weights):
    nc = K.nc
    K.ones = K.sb("ones", [P, P])
    K.ident = K.sb("ident", [P, P])
    K.cols = K.sb("param_cols", [P, P])
    loaded, turned, copied, made = (K.sem("start_" + n) for n in ("loaded", "turned", "copied", "made"))
    K.at, rows = {}, []

    def row(name, ap):
        K.at[name] = sum(a.shape[0] for _, a in rows)
        rows.append((K.at[name], ap))
    row("norm_ab", I["mix_norm_ab"].rearrange("a (c p) -> (a c) p", p=P))
    row("norm_ret", I["mix_norm_ret"].rearrange("a (c p) -> (a c) p", p=P))
    row("norm_ffn", I["ffn_norm"].rearrange("a (c p) -> (a c) p", p=P))
    row("norm_mix_2", I["norm_mix_2"].rearrange("a (c p) -> (a c) p", p=P))
    row("norm_ffn_2", I["norm_ffn_2"].rearrange("a (c p) -> (a c) p", p=P))
    row("conv_w", I["lru_conv_w"].rearrange("a j (c p) -> (a j c) p", p=P))
    row("conv_b", I["lru_conv_b"].rearrange("a (c p) -> (a c) p", p=P))
    row("b_a", I["lru_b_a"].rearrange("a (c two) d -> (a c) (two d)", two=2))
    row("b_i", I["lru_b_i"].rearrange("a (c two) d -> (a c) (two d)", two=2))
    row("lambda", I["lru_lambda"].rearrange("a (c p) -> (a c) p", p=P))
    row("cond", I["c_2"].rearrange("a (c p) -> (a c) p", p=P))
    row("out_norm", I["gdn_out_norm_2"])
    n_rows = K.at["out_norm"] + 1
    for name, src in (("q_norm", "q_norm"), ("k_norm", "k_norm"), ("dsw_q_norm", "dsw_q_norm_2"),
                      ("dsw_k_norm", "dsw_k_norm_2")):
        K.at[name] = n_rows
        rows.append((n_rows, I[src]))
        n_rows += 1
    with ExitStack() as ctx:
        tok = K.sb("x_tokens", [P, QB, D], ctx=ctx)
        meta = K.sb("meta_tokens", [N_META, D], ctx=ctx)
        prow = K.sb("param_rows", [P, P], ctx=ctx)
        tick = K.sb("tick", [P, 12], ctx=ctx)
        n_loads = 0
        with nc.Block() as block:
            @block.sync
            def _(sp):
                nonlocal n_loads
                pairs = [(K.ident[:], K.const["ident"][:]), (meta[:], I["meta_tokens"])]
                for at, ap in rows:
                    if ap.shape[-1] == HD:
                        pairs += [(prow[at:at + 1, h * HD:(h + 1) * HD], ap) for h in range(2)]
                    else:
                        pairs.append((prow[at:at + ap.shape[0], :], ap))
                pairs.append((tok[:], I["x"].rearrange("a (b p) f -> p (a b) f", p=P)))
                load_all(K, sp, pairs, loaded)
                for j in range(2):
                    K.load(sp, *first_tile(first_weights, j))
                n_loads = 16 * len(pairs)

            @block.gpsimd
            def _(pool):
                nc.gpsimd.memset(K.ones[:], 1.0).then_inc(made, 1)
                for n, s in enumerate((K.tile_used, K.psum_free, K.hi_ready, K.lo_ready, K.up["product"][0],
                                       K.up["lo"][0])):
                    for m in range(2):
                        nc.gpsimd.memset(tick[:, 2 * n + m:2 * n + m + 1], 0.0).then_inc(s, 1)

            @block.tensor
            def _(pe):
                pe.wait_ge(loaded, n_loads)
                for c in range(DC):
                    for b in range(QB):
                        mm = nc.tensor.transpose(K.ps[:, c, b * P:(b + 1) * P], tok[:, b, c * P:(c + 1) * P], K.ident[:])
                    mm.then_inc(turned, 1)
                pe.wait_ge(copied, 2)
                for c in range(DC):
                    mm = nc.tensor.transpose(K.ps[:, 0, c * N_META:(c + 1) * N_META], meta[:, c * P:(c + 1) * P],
                                             K.ident[0:N_META, 0:N_META])
                mm = nc.tensor.transpose(K.ps[:, 1, 0:n_rows], prow[0:n_rows, :], K.ident[0:n_rows, 0:n_rows])
                mm.then_inc(turned, 1)

            @block.scalar
            def _(act):
                for c in range(DC):
                    act.wait_ge(turned, c + 1)
                    nc.scalar.activation(K.x[:, c, N_META:T], K.ps[:, c, :], ACT.Copy).then_inc(copied, 1)
                act.wait_ge(turned, DC + 1)
                nc.scalar.activation(K.x[:, :, 0:N_META],
                                     K.ps[:, 0, 0:DC * N_META].rearrange("p (c t) -> p c t", c=DC), ACT.Copy)
                nc.scalar.activation(K.cols[:, 0:n_rows], K.ps[:, 1, 0:n_rows], ACT.Copy)
                K.split_hi(act, first_weights, 0, 0)

            @block.vector
            def _(dve):
                K.split_lo(dve, first_weights, 0, 0)


def first_tile(w, j):
    return (w, 0, j) if j < w.tiles else (w.next, 0, j - w.tiles)


def param(K, name, n):
    at = K.at[name]
    return K.cols[:, at:at + n]


def log1p_chain(K, dve, out, z, t1, t2):
    nc, link = K.nc, K.dve.link
    link(dve, nc.vector.tensor_scalar(t1, z, 2.0, None, ALU.add))
    link(dve, nc.vector.reciprocal(t1, t1))
    link(dve, nc.vector.tensor_tensor(t1, t1, z, ALU.mult))
    link(dve, nc.vector.tensor_tensor(t2, t1, t1, ALU.mult))
    link(dve, nc.vector.tensor_scalar(out, t2, 1.0 / 15, None, ALU.mult))
    for n in (13, 11, 9, 7, 5, 3):
        link(dve, nc.vector.scalar_tensor_tensor(out, out, 1.0 / n, t2, ALU.add, ALU.mult))
    link(dve, nc.vector.scalar_tensor_tensor(out, out, 1.0, t1, ALU.add, ALU.mult))
    link(dve, nc.vector.tensor_scalar(out, out, 2.0, None, ALU.mult))


def rg_lru(K, I, proj):
    nc = K.nc
    S = {n: K.sem("lru_" + n) for n in ("loaded", "cleared", "conv", "gates", "read", "decay", "ez", "rate",
                                        "squares", "mult", "gelu", "y", "y_hi")}
    conv_w, conv_b = param(K, "conv_w", 16), param(K, "conv_b", 4)
    with ExitStack() as ctx:
        xc = K.sb("conv_out", [P, LRU_CH, T], ctx=ctx)
        r = K.sb("lru_r", [P, LRU_CH, T], ctx=ctx)
        ig = K.sb("lru_i", [P, LRU_CH, T], ctx=ctx)
        s = K.sb("lru_s", [P, LRU_CH, T], ctx=ctx)
        wg = K.sb("lru_gate_w", [P, 2, LRU_CH, P], ctx=ctx)
        small = K.sb("lru_small", [P, 6, LRU_CH], ctx=ctx)
        rate, minus_rate, ez = small[:, 0, :], small[:, 1, :], small[:, 2, :]
        with nc.Block() as block:
            @block.gpsimd
            def _(pool):
                nc.gpsimd.memset(wg[:], 0.0).then_inc(S["cleared"], 1)

            @block.sync
            def _(sp):
                sp.wait_ge(S["cleared"], 1)
                for g, name in enumerate(("lru_w_a", "lru_w_i")):
                    pairs = I[name].rearrange("a (c two) i j -> two i (a c) j", two=2)
                    for h in range(2):
                        sp.dma_start(wg[h * HD:(h + 1) * HD, g, :, h * HD:(h + 1) * HD], pairs[h])\
                            .then_inc(S["loaded"], 16)

            @block.tensor
            def _(pe):
                pe.wait_ge(S["loaded"], 64)
                for c in range(LRU_CH):
                    pe.wait_ge(S["conv"], c + 1)
                    if c >= 2:
                        pe.wait_ge(S["read"], 2 * (c - 1))
                    for g in range(2):
                        for h in range(2):
                            mm = nc.tensor.matmul(K.ps[:, (c % 2) * 4 + g * 2 + h, 0:T // 2], wg[:, g, c, :],
                                                  xc[:, c, h * (T // 2):(h + 1) * (T // 2)], start=True, stop=True)
                    mm.then_inc(S["gates"], 1)

            @block.scalar
            def _(act):
                nc.scalar.activation(small[:, 3, :], param(K, "lambda", 4), ACT.Abs).then_inc(K.act.sem, 1)
                K.act.n += 1
                act.wait_ge(K.act.sem, K.act.n)
                nc.scalar.activation(ez, small[:, 3, :], ACT.Exp, scale=-1.0).then_inc(S["ez"], 1)
                for c in range(LRU_CH):
                    act.wait_ge(S["gates"], c + 1)
                    for g, (buf, bias) in enumerate(((r, "b_a"), (ig, "b_i"))):
                        b = (c % 2) * 4 + g * 2
                        nc.scalar.activation(K.spans(buf[:, c, :], ALL), K.ps[:, b:b + 2, 0:T // 2], ACT.Sigmoid,
                                             bias=param(K, bias, 4)[:, c:c + 1]).then_inc(S["read"], 1)
                act.wait_ge(S["rate"], 1)
                act.wait_ge(S["read"], 2 * LRU_CH)
                for c in range(LRU_CH):
                    nc.scalar.activation(s[:, c, :], r[:, c, :], ACT.Tanh, scale=rate[:, c:c + 1])\
                        .then_inc(S["decay"], 1)
                for c in range(LRU_CH):
                    act.wait_ge(S["decay"], c + 1)
                    nc.scalar.activation(r[:, c, :], r[:, c, :], ACT.Exp, scale=minus_rate[:, c:c + 1])\
                        .then_inc(S["decay"], 1)
                act.wait_ge(S["squares"], 1)
                nc.scalar.activation(s[:], s[:], ACT.Sqrt).then_inc(S["mult"], 1)
                nc.scalar.activation(proj[:, 4:8, :], proj[:, 4:8, :], ACT.Gelu_apprx_tanh).then_inc(S["gelu"], 1)
                act.wait_ge(S["y"], 1)
                nc.scalar.activation(K.h_hi[:, 0:4, :], s[:], ACT.Copy).then_inc(S["y_hi"], 1)

            @block.vector
            def _(dve):
                link = K.dve.link
                for c in range(LRU_CH):
                    link(dve, nc.vector.tensor_scalar(xc[:, c, :], proj[:, c, :], conv_w[:, 12 + c:13 + c],
                                                      conv_b[:, c:c + 1], ALU.mult, ALU.add))
                    for back in (1, 2, 3):
                        tap = conv_w[:, (3 - back) * 4 + c:(3 - back) * 4 + c + 1]
                        ins = nc.vector.scalar_tensor_tensor(xc[:, c, back:T], proj[:, c, 0:T - back], tap,
                                                             xc[:, c, back:T], ALU.mult, ALU.add)
                        if back < 3:
                            link(dve, ins)
                    ins.then_inc(S["conv"], 1)
                dve.wait_ge(S["ez"], 1)
                log1p_chain(K, dve, rate, ez, small[:, 4, :], small[:, 5, :])
                link(dve, nc.vector.tensor_scalar(minus_rate, param(K, "lambda", 4), -1.0, 0.0, ALU.mult, ALU.max))
                link(dve, nc.vector.tensor_tensor(rate, rate, minus_rate, ALU.add))
                link(dve, nc.vector.tensor_scalar(rate, rate, LRU_C, None, ALU.mult))
                nc.vector.tensor_scalar(minus_rate, rate, -1.0, None, ALU.mult).then_inc(S["rate"], 1)
                dve.wait_ge(S["read"], 2 * LRU_CH)
                link(dve, nc.vector.tensor_tensor(ig[:], ig[:], xc[:], ALU.mult))
                dve.wait_ge(S["decay"], LRU_CH)
                link(dve, nc.vector.tensor_scalar(xc[:], s[:], 1.0, None, ALU.add))
                link(dve, nc.vector.reciprocal(xc[:], xc[:]))
                nc.vector.scalar_tensor_tensor(s[:], s[:], 2.0, xc[:], ALU.mult, ALU.mult).then_inc(S["squares"], 1)
                dve.wait_ge(S["mult"], 1)
                link(dve, nc.vector.memset(s[:, :, 0:1], 1.0))
                link(dve, nc.vector.tensor_tensor(ig[:], ig[:], s[:], ALU.mult))
                dve.wait_ge(S["decay"], 2 * LRU_CH)
                for c in range(LRU_CH):
                    link(dve, nc.vector.tensor_tensor_scan(xc[:, c, :], r[:, c, :], ig[:, c, :], 0.0,
                                                           ALU.mult, ALU.add))
                dve.wait_ge(S["gelu"], 1)
                nc.vector.tensor_tensor(s[:], xc[:], proj[:, 4:8, :], ALU.mult).then_inc(S["y"], 1)
                dve.wait_ge(S["y_hi"], 1)
                nc.vector.tensor_tensor(K.h_lo[:, 0:4, :], s[:], K.h_hi[:, 0:4, :].bitcast(F32), ALU.subtract)


def head_norm(K, name, parts, sum_over, scale):
    nc = K.nc
    S = {n: K.sem(name + "_" + n) for n in ("squares", "sums", "var", "std", "scaled")}
    W = T
    with ExitStack() as ctx:
        sq = K.sb(name + "_sq", [P, 2, 4 * SEQ + 64], ctx=ctx)
        rs = K.sb(name + "_rs", [P, 2, 4 * SEQ + 64], ctx=ctx)

        def flat(buf, n, v):
            chunks, w = v.shape[1], v.shape[2]
            return buf[:, n % 2, 0:chunks * w].rearrange("p (c w) -> p c w", c=chunks)

        def spans_of(v):
            return 1 if v.shape[2] <= 512 else 2

        def banks(n, v):
            s = spans_of(v)
            return K.ps[:, (n % 2) * 4:(n % 2) * 4 + v.shape[1] * s, 0:v.shape[2] // s]

        def by_span(buf, n, v):
            s = spans_of(v)
            return buf[:, n % 2, 0:v.shape[1] * v.shape[2]].rearrange("p (b w) -> p b w", b=v.shape[1] * s)

        with nc.Block() as block:
            @block.scalar
            def _(act):
                def square(n):
                    v = parts[n][0]
                    if n >= 2:
                        act.wait_ge(S["sums"], n - 1)
                    nc.scalar.activation(flat(sq, n, v), v, ACT.Square).then_inc(S["squares"], 1)
                square(0)
                for n, (v, _) in enumerate(parts):
                    if n + 1 < len(parts):
                        square(n + 1)
                    act.wait_ge(S["var"], n + 1)
                    nc.scalar.activation(flat(rs, n, v), flat(rs, n, v), ACT.Sqrt).then_inc(S["std"], 1)

            @block.tensor
            def _(pe):
                for n, (v, _) in enumerate(parts):
                    pe.wait_ge(S["squares"], n + 1)
                    if n >= 2:
                        pe.wait_ge(S["var"], n - 1)
                    b, q = banks(n, v), by_span(sq, n, v)
                    for m in range(b.shape[1]):
                        mm = nc.tensor.matmul(b[:, m, :], sum_over, q[:, m, :], start=True, stop=True)
                    mm.then_inc(S["sums"], 1)

            @block.vector
            def _(dve):
                def var(n):
                    v = parts[n][0]
                    dve.wait_ge(S["sums"], n + 1)
                    nc.vector.tensor_scalar(by_span(rs, n, v), banks(n, v), scale, EPS, ALU.mult, ALU.add)\
                        .then_inc(S["var"], 1)
                var(0)
                for n, (v, gain) in enumerate(parts):
                    if n + 1 < len(parts):
                        if n >= 1:
                            dve.wait_ge(S["scaled"], n)
                        var(n + 1)
                    dve.wait_ge(S["std"], n + 1)
                    K.dve.link(dve, nc.vector.reciprocal(flat(rs, n, v), flat(rs, n, v)))
                    nc.vector.scalar_tensor_tensor(v, v, gain, flat(rs, n, v), ALU.mult, ALU.mult)\
                        .then_inc(S["scaled"], 1)


def rotate_heads(K, chunks, turn, cos, sin, tmp, name):
    nc = K.nc
    S = {n: K.sem(name + "_" + n) for n in ("turned", "first", "sum")}
    with nc.Block() as block:
        @block.tensor
        def _(pe):
            for n, v in enumerate(chunks):
                if n >= 2:
                    pe.wait_ge(S["first"], n - 1)
                for s in range(2):
                    mm = nc.tensor.matmul(K.ps[:, (n % 2) * 2 + s, 0:T // 2], turn,
                                          v[:, s * (T // 2):(s + 1) * (T // 2)], start=True, stop=True)
                mm.then_inc(S["turned"], 1)

        @block.vector
        def _(dve):
            for n, v in enumerate(chunks):
                dve.wait_ge(S["turned"], n + 1)
                nc.vector.tensor_tensor(K.spans(tmp, ALL), K.ps[:, (n % 2) * 2:(n % 2) * 2 + 2, 0:T // 2],
                                        K.spans(sin, ALL), ALU.mult).then_inc(S["first"], 1)
                K.dve.link(dve, nc.vector.tensor_tensor(v, v, cos, ALU.mult))
                dve.wait_ge(S["first"], n + 1)
                K.dve.link(dve, nc.vector.tensor_tensor(v, v, tmp, ALU.add))


def window_attention(K, I, q, k, v, v_meta):
    nc = K.nc
    scale = HD ** -0.5
    with ExitStack() as ctx:
        load = K.sem("att_loaded")
        cos = K.sb("att_cos", [P, T], ctx=ctx)
        sin = K.sb("att_sin", [P, T], ctx=ctx)
        turn = K.sb("att_turn", [P, P], ctx=ctx)
        head_ones = K.sb("att_head_ones", [P, P], ctx=ctx)
        mask = K.sb("window_mask", [P, N_META + 2 * P], ctx=ctx)
        mask0 = K.sb("first_mask", [P, N_META + P], ctx=ctx)
        mask_meta = K.sb("meta_mask", [N_META, N_META], ctx=ctx)
        sink = K.sb("sinks", [P, ATT_HEADS], ctx=ctx)
        k2 = K.sb("k_both", [P, 2, T], ctx=ctx)
        with nc.Block() as block:
            @block.sync
            def _(sp):
                pairs = [(cos, "att_cos"), (sin, "att_sin"), (turn, "turn"), (head_ones, "head_ones"),
                         (mask, "window_mask"), (mask0, "first_mask"), (mask_meta, "meta_mask")]
                load_all(K, sp, [(t[:], K.const[n][:]) for t, n in pairs], load)
                sp.dma_start(sink[:], I["attn_sinks"].to_broadcast([P, ATT_HEADS])).then_inc(load, 16)
                sp.wait_ge(load, 16 * (len(pairs) + 1))
        with ExitStack() as inner:
            head_norm(K, "att_norm", [(q[:, 0:2, :], param(K, "q_norm", 1)), (q[:, 2:4, :], param(K, "q_norm", 1)),
                                      (k[:, 0:1, :], param(K, "k_norm", 1))], head_ones[:], 1.0 / HD)
            tmp = K.sb("att_rot", [P, T], ctx=inner)
            rotate_heads(K, [q[:, c, :] for c in range(4)] + [k[:, 0, :]], turn[:], cos[:], sin[:], tmp[:], "att_rope")
        copied = K.sem("att_keys_copied")
        with nc.Block() as block:
            @block.sync
            def _(sp):
                for g in range(2):
                    for h in range(2):
                        sp.dma_start(k2[h * HD:(h + 1) * HD, g, :], k[g * HD:(g + 1) * HD, 0, :])\
                            .then_inc(copied, 16)
                sp.wait_ge(copied, 64)
        S = {n: K.sem("att_" + n) for n in ("scores", "masked", "max", "exp", "probs", "turned", "turned_read",
                                            "out", "out_hi", "out_lo")}
        s = K.sb("att_s", [P, 4, N_META + 2 * P], ctx=ctx)
        pt = K.sb("att_pt", [P, 2, 2 * P], ctx=ctx)
        pt_meta = K.sb("att_pt_meta", [N_META, 2, P], ctx=ctx)
        st = K.sb("att_stats", [P, 6, 4], ctx=ctx)
        top, minus, esink, total = (st[:, n, :] for n in range(4))
        steps = [(b, g) for b in range(QB) for g in range(2)]

        def nk(b):
            return N_META + P if b == 0 else N_META + 2 * P

        def output_rest(dve, n):
            b, g = steps[n]
            at = slice(N_META + b * P, N_META + (b + 1) * P)
            dve.wait_ge(S["out_hi"], n + 1)
            nc.vector.tensor_tensor(K.h_lo[:, 4 + 2 * g:6 + 2 * g, at],
                                    K.ps[:, 6 + n % 2, 0:2 * P].rearrange("p (c w) -> p c w", c=2),
                                    K.h_hi[:, 4 + 2 * g:6 + 2 * g, at].bitcast(F32), ALU.subtract)\
                .then_inc(S["out_lo"], 1)

        with nc.Block() as block:
            @block.tensor
            def _(pe):
                for n, (b, g) in enumerate(steps):
                    if n >= 1:
                        pe.wait_ge(S["masked"], n)
                    own = slice(N_META + b * P, N_META + (b + 1) * P)
                    for u in range(4):
                        half = slice((u % 2) * HD, (u % 2 + 1) * HD)
                        query = q[half, 2 * g + u // 2, own]
                        if b <= 1:
                            mm = nc.tensor.matmul(K.ps[:, u, 0:nk(b)], query, k2[half, g, 0:nk(b)],
                                                  start=True, stop=True)
                        else:
                            nc.tensor.matmul(K.ps[:, u, 0:N_META], query, k2[half, g, 0:N_META],
                                             start=True, stop=True)
                            mm = nc.tensor.matmul(K.ps[:, u, N_META:nk(b)], query,
                                                  k2[half, g, N_META + (b - 1) * P:N_META + (b + 1) * P],
                                                  start=True, stop=True)
                    mm.then_inc(S["scores"], 1)
                    pe.wait_ge(S["probs"], n + 1)
                    if n >= 2:
                        pe.wait_ge(S["out_lo"], n - 1)
                    for u in range(4):
                        e = 4 * n + u
                        if e >= 2:
                            pe.wait_ge(S["turned_read"], e - 1)
                        nc.tensor.transpose(K.ps[0:N_META, 4 + u % 2, 0:P], s[:, u, 0:N_META], K.ident[:])
                        for m in range(nk(b) // P):
                            mm = nc.tensor.transpose(K.ps[:, 4 + u % 2, (m + 1) * P:(m + 2) * P],
                                                     s[:, u, N_META + m * P:N_META + (m + 1) * P], K.ident[:])
                        mm.then_inc(S["turned"], 1)
                        pe.wait_ge(S["turned_read"], e + 1)
                        out = K.ps[(u % 2) * HD:(u % 2 + 1) * HD, 6 + n % 2, (u // 2) * P:(u // 2 + 1) * P]
                        dv = slice(g * HD, (g + 1) * HD)
                        nc.tensor.matmul(out, v_meta[:, dv], pt_meta[:, u % 2, :], start=True, stop=False)
                        blocks = [b] if b == 0 else [b - 1, b]
                        for m, kb in enumerate(blocks):
                            mm = nc.tensor.matmul(out, v[:, kb, dv], pt[:, u % 2, m * P:(m + 1) * P],
                                                  start=False, stop=m == len(blocks) - 1)
                    mm.then_inc(S["out"], 1)

            @block.vector
            def _(dve):
                link = K.dve.link
                for n, (b, g) in enumerate(steps):
                    m = (mask0 if b == 0 else mask)[:, 0:nk(b)].unsqueeze(1).to_broadcast([P, 4, nk(b)])
                    sv = s[:, :, 0:nk(b)]
                    snk = sink[:, 4 * g:4 * g + 4]
                    dve.wait_ge(S["scores"], n + 1)
                    if n >= 1:
                        dve.wait_ge(S["turned"], 4 * n)
                    nc.vector.scalar_tensor_tensor(sv, K.ps[:, 0:4, 0:nk(b)], scale, m, ALU.mult, ALU.add)\
                        .then_inc(S["masked"], 1)
                    dve.wait_ge(S["masked"], n + 1)
                    link(dve, nc.vector.tensor_reduce(top, sv, AX_X, ALU.max))
                    link(dve, nc.vector.tensor_tensor(top, top, snk, ALU.max))
                    link(dve, nc.vector.tensor_scalar(minus, top, -1.0, None, ALU.mult))
                    nc.vector.tensor_tensor(esink, snk, minus, ALU.add).then_inc(S["max"], 1)
                    if n >= 1:
                        output_rest(dve, n - 1)
                    dve.wait_ge(S["exp"], n + 1)
                    link(dve, nc.vector.tensor_tensor(total, total, esink, ALU.add))
                    link(dve, nc.vector.reciprocal(total, total))
                    nc.vector.tensor_tensor(sv, sv, total.unsqueeze(2).to_broadcast([P, 4, nk(b)]), ALU.mult)\
                        .then_inc(S["probs"], 1)
                output_rest(dve, len(steps) - 1)

            @block.scalar
            def _(act):
                for n, (b, g) in enumerate(steps):
                    act.wait_ge(S["max"], n + 1)
                    for u in range(4):
                        nc.scalar.activation(s[:, u, 0:nk(b)], s[:, u, 0:nk(b)], ACT.Exp, bias=minus[:, u:u + 1],
                                             accum_out=total[:, u:u + 1])
                    nc.scalar.activation(esink, esink, ACT.Exp).then_inc(S["exp"], 1)
                    for u in range(4):
                        e = 4 * n + u
                        act.wait_ge(S["turned"], e + 1)
                        nc.scalar.activation(pt_meta[:, u % 2, :], K.ps[0:N_META, 4 + u % 2, 0:P], ACT.Copy)
                        nc.scalar.activation(pt[:, u % 2, 0:nk(b) - N_META],
                                             K.ps[:, 4 + u % 2, P:P + nk(b) - N_META], ACT.Copy)\
                            .then_inc(S["turned_read"], 1)
                    act.wait_ge(S["out"], n + 1)
                    at = slice(N_META + b * P, N_META + (b + 1) * P)
                    nc.scalar.activation(K.h_hi[:, 4 + 2 * g:6 + 2 * g, at],
                                         K.ps[:, 6 + n % 2, 0:2 * P].rearrange("p (c w) -> p c w", c=2),
                                         ACT.Copy).then_inc(S["out_hi"], 1)
        M = {n: K.sem("att_meta_" + n) for n in ("scores", "shifted", "exp", "probs", "turned", "read", "out", "hi")}
        ms = K.sb("att_meta_s", [N_META, ATT_HEADS, N_META], ctx=ctx)
        mt = K.sb("att_meta_t", [N_META, ATT_HEADS, N_META], ctx=ctx)
        mst = K.sb("att_meta_stats", [N_META, 4, ATT_HEADS], ctx=ctx)
        mtop, mtotal, msink = (mst[:, n, :] for n in range(3))
        wide = [N_META, ATT_HEADS, N_META]
        place = [(h % 2) * 4 + h // 2 for h in range(ATT_HEADS)]
        msinks = sink[0:N_META, :].rearrange("p (c two) -> p two c", two=2)
        meta_out = K.ps[:, 2, 0:4 * N_META].rearrange("p (c t) -> p c t", c=4)
        with nc.Block() as block:
            @block.tensor
            def _(pe):
                def scores_at(h):
                    return K.ps[0:N_META, 3 * (h % 2), (h // 2) * N_META:(h // 2 + 1) * N_META]
                for h in range(ATT_HEADS):
                    half = slice((h % 2) * HD, (h % 2 + 1) * HD)
                    mm = nc.tensor.matmul(scores_at(h), q[half, h // 2, 0:N_META], k2[half, h // 4, 0:N_META],
                                          start=True, stop=True)
                mm.then_inc(M["scores"], 1)
                pe.wait_ge(M["probs"], 1)
                for h in range(ATT_HEADS):
                    mm = nc.tensor.transpose(K.ps[0:N_META, 1, h * N_META:(h + 1) * N_META], ms[:, h, :],
                                             K.ident[0:N_META, 0:N_META])
                mm.then_inc(M["turned"], 1)
                pe.wait_ge(M["read"], 1)
                for h in range(ATT_HEADS):
                    g = h // 4
                    mm = nc.tensor.matmul(K.ps[(h % 2) * HD:(h % 2 + 1) * HD, 2, (h // 2) * N_META:(h // 2 + 1) * N_META],
                                          v_meta[:, g * HD:(g + 1) * HD], mt[:, place[h], :], start=True, stop=True)
                mm.then_inc(M["out"], 1)

            @block.vector
            def _(dve):
                link = K.dve.link
                dve.wait_ge(M["scores"], 1)
                for odd in range(2):
                    link(dve, nc.vector.scalar_tensor_tensor(
                        ms[:, 4 * odd:4 * odd + 4, :],
                        K.ps[0:N_META, 3 * odd, 0:4 * N_META].rearrange("p (h k) -> p h k", h=4), scale,
                        mask_meta[:].unsqueeze(1).to_broadcast([N_META, 4, N_META]), ALU.mult, ALU.add))
                link(dve, nc.vector.tensor_reduce(mtop, ms[:], AX_X, ALU.max))
                by_parity = mtop.rearrange("p (two c) -> p two c", two=2)
                link(dve, nc.vector.tensor_tensor(by_parity, by_parity, msinks, ALU.max))
                link(dve, nc.vector.tensor_tensor(ms[:], ms[:], mtop.unsqueeze(2).to_broadcast(wide), ALU.subtract))
                nc.vector.tensor_tensor(msink.rearrange("p (two c) -> p two c", two=2), msinks, by_parity, ALU.subtract).then_inc(M["shifted"], 1)
                dve.wait_ge(M["exp"], 1)
                link(dve, nc.vector.tensor_reduce(mtotal, ms[:], AX_X, ALU.add))
                link(dve, nc.vector.tensor_tensor(mtotal, mtotal, msink, ALU.add))
                link(dve, nc.vector.reciprocal(mtotal, mtotal))
                nc.vector.tensor_tensor(ms[:], ms[:], mtotal.unsqueeze(2).to_broadcast(wide), ALU.mult)\
                    .then_inc(M["probs"], 1)
                dve.wait_ge(M["hi"], 1)
                nc.vector.tensor_tensor(K.h_lo[:, 4:8, 0:N_META], meta_out, K.h_hi[:, 4:8, 0:N_META].bitcast(F32),
                                        ALU.subtract)

            @block.scalar
            def _(act):
                act.wait_ge(M["shifted"], 1)
                nc.scalar.activation(ms[:], ms[:], ACT.Exp)
                nc.scalar.activation(msink, msink, ACT.Exp).then_inc(M["exp"], 1)
                act.wait_ge(M["turned"], 1)
                nc.scalar.activation(mt[:], K.ps[0:N_META, 1, 0:ATT_HEADS * N_META]
                                     .rearrange("p (h k) -> p h k", h=ATT_HEADS), ACT.Copy).then_inc(M["read"], 1)
                act.wait_ge(M["out"], 1)
                nc.scalar.activation(K.h_hi[:, 4:8, 0:N_META], meta_out, ACT.Copy).then_inc(M["hi"], 1)


def retention(K, W):
    nc = K.nc
    with ExitStack() as layer:
        o = K.sb("ret_o", [P, 4 * RET_HEADS, SEQ], ctx=layer)
        K.take_h("ret_h", layer)
        normalize(K, ALL, param(K, "norm_ret", 8))
        with ExitStack() as heads:
            q = K.sb("ret_q_t", [P, 2 * RET_HEADS, SEQ], ctx=heads)
            k = K.sb("ret_k_t", [P, 2 * RET_HEADS, T], ctx=heads)
            project(K, W["ret_q"], q, ONLY_X, base=N_META)
            project(K, W["ret_k"], k, ALL)
            rotate_retention(K, q, k)
            v = K.sb("ret_v", [P, QB, 2 * RET_V], ctx=heads)
            v_meta = K.sb("ret_v_meta", [N_META, 2 * RET_V], ctx=heads)
            for pair in range(2):
                project_tokens(K, W["ret_v%d" % pair], *token_blocks(v, v_meta, 256))
                retention_heads(K, pair, q, k, v, v_meta, o)
        y = [K.sb("ret_y_" + n, [P, 4 * RET_HEADS, SEQ], F32R, layer) for n in ("hi", "lo")]
        gate_and_project(K, W["ret_g"], o, y)
        add_projected(K, W["ret_out"], y, ONLY_X, base=N_META)


def rotate_retention(K, q, k):
    nc = K.nc
    loaded = K.sem("ret_tables_loaded")
    with ExitStack() as ctx:
        cos = K.sb("ret_cos", [P, T], ctx=ctx)
        sin = K.sb("ret_sin", [P, T], ctx=ctx)

        def turn(eng, engine, chain, buf, first, name):
            w = T - first
            wide = [P, 2, w]
            c = cos[:, first:T].unsqueeze(1).to_broadcast(wide)
            s = sin[:, first:T].unsqueeze(1).to_broadcast(wide)
            pairs = buf[:].rearrange("p (h two) w -> p two h w", two=2)
            eng.wait_ge(loaded, 32)
            for g in range(2):
                a, b = pairs[:, 0, 2 * g:2 * g + 2, :], pairs[:, 1, 2 * g:2 * g + 2, :]
                ta, tb = tmp[name][0][:, :, 0:w], tmp[name][1][:, :, 0:w]
                for dst, x, y, op in ((ta, a, s, ALU.mult), (tb, b, s, ALU.mult), (a, a, c, ALU.mult),
                                      (b, b, c, ALU.mult), (a, a, tb, ALU.subtract), (b, b, ta, ALU.add)):
                    chain.link(eng, engine.tensor_tensor(dst, x, y, op))
        tmp = {n: [K.sb("ret_rot_%s%d" % (n, m), [P, 2, T], ctx=ctx) for m in range(2)] for n in "qk"}
        with nc.Block() as block:
            @block.sync
            def _(sp):
                load_all(K, sp, [(cos[:], K.const["ret_cos"][:]), (sin[:], K.const["ret_sin"][:])], loaded)

            @block.vector
            def _(dve):
                turn(dve, nc.vector, K.dve, q, N_META, "q")

            @block.gpsimd
            def _(pool):
                turn(pool, nc.gpsimd, K.pool, k, 0, "k")


def retention_heads(K, pair, q, k, v, v_meta, o):
    nc = K.nc
    S = {n: K.sem("ret%d_%s" % (pair, n)) for n in
         ("loaded", "scores", "probs", "out", "kept", "summed", "total", "var", "std", "scaled")}
    heads = (2 * pair, 2 * pair + 1)
    NV = RET_V // P
    with ExitStack() as ctx:
        decay = K.sb("ret_decay%d" % pair, [P, 2, SEQ], ctx=ctx)
        decay_meta = K.sb("ret_decay_meta%d" % pair, [N_META, 2, SEQ], ctx=ctx)
        pt = [K.sb("ret_p%d_%d" % (pair, b), [P, SEQ - b * P], ctx=ctx) for b in range(QB)]
        pt_meta = K.sb("ret_p%d_meta" % pair, [N_META, SEQ], ctx=ctx)
        sq = K.sb("ret_sq%d" % pair, [P, NV, SEQ], ctx=ctx)
        rs = sq[:, 3, :]
        with nc.Block() as block:
            @block.sync
            def _(sp):
                at = slice(heads[0] * SEQ, (heads[1] + 1) * SEQ)
                load_all(K, sp, [
                    (decay[:].rearrange("p h w -> p (h w)"), K.const["ret_decay"][:, at]),
                    (decay_meta[:].rearrange("p h w -> p (h w)"), K.const["ret_decay_meta"][:, at])], S["loaded"])

            @block.tensor
            def _(pe):
                for n, h in enumerate(heads):
                    if n:
                        pe.wait_ge(S["probs"], 5 * n)
                    for d in range(2):
                        c = 2 * h + d
                        for b in range(QB):
                            mm = nc.tensor.matmul(K.ps[:, b, 0:SEQ - b * P], k[:, c, N_META + b * P:N_META + (b + 1) * P],
                                                  q[:, c, b * P:SEQ], start=d == 0, stop=d == 1)
                            if d:
                                mm.then_inc(S["scores"], 1)
                        mm = nc.tensor.matmul(K.ps[0:N_META, 4, :], k[:, c, 0:N_META], q[:, c, :],
                                              start=d == 0, stop=d == 1)
                    mm.then_inc(S["scores"], 1)
                    pe.wait_ge(S["probs"], 5 * (n + 1))
                    for m in range(NV):
                        e = n * NV + m
                        bank = 5 + e % 3
                        if e >= 3:
                            pe.wait_ge(S["kept"], e - 2)
                        cols = slice(n * RET_V + m * P, n * RET_V + (m + 1) * P)
                        nc.tensor.matmul(K.ps[:, bank, :], v_meta[:, cols], pt_meta[:], start=True, stop=False)
                        for b in range(QB):
                            mm = nc.tensor.matmul(K.ps[:, bank, b * P:SEQ], v[:, b, cols], pt[b][:],
                                                  start=False, stop=b == QB - 1)
                        mm.then_inc(S["out"], 1)
                    pe.wait_ge(S["summed"], n + 1)
                    nc.tensor.matmul(K.ps[:, 4, :], K.ones[:], sq[:, 0, :], start=True, stop=True)\
                        .then_inc(S["total"], 1)
                    if n == 0:
                        pe.wait_ge(S["var"], 1)

            @block.scalar
            def _(act):
                for n, h in enumerate(heads):
                    for m in range(NV):
                        e = n * NV + m
                        act.wait_ge(S["out"], e + 1)
                        if n and m == 0:
                            act.wait_ge(S["scaled"], n)
                        nc.scalar.activation(sq[:, m, :], K.ps[:, 5 + e % 3, :], ACT.Square)
                        nc.scalar.activation(o[:, h * NV + m, :], K.ps[:, 5 + e % 3, :], ACT.Copy)\
                            .then_inc(S["kept"], 1)
                    act.wait_ge(S["var"], n + 1)
                    nc.scalar.activation(rs, rs, ACT.Sqrt).then_inc(S["std"], 1)

            @block.vector
            def _(dve):
                link = K.dve.link
                dve.wait_ge(S["loaded"], 32)
                for n, h in enumerate(heads):
                    for b in range(QB + 1):
                        dve.wait_ge(S["scores"], 5 * n + b + 1)
                        if n and b == 0:
                            dve.wait_ge(S["out"], NV * n)
                        if b < QB:
                            dst, src, by = pt[b][:], K.ps[:, b, 0:SEQ - b * P], decay[:, n, 0:SEQ - b * P]
                        else:
                            dst, src, by = pt_meta[:], K.ps[0:N_META, 4, :], decay_meta[:, n, :]
                        nc.vector.scalar_tensor_tensor(dst, src, (2 * P) ** -0.5, by, ALU.mult, ALU.mult)\
                            .then_inc(S["probs"], 1)
                    dve.wait_ge(S["kept"], NV * (n + 1))
                    link(dve, nc.vector.tensor_tensor(sq[:, 0:2, :], sq[:, 0:2, :], sq[:, 2:4, :], ALU.add))
                    nc.vector.tensor_tensor(sq[:, 0, :], sq[:, 0, :], sq[:, 1, :], ALU.add).then_inc(S["summed"], 1)
                    dve.wait_ge(S["total"], n + 1)
                    nc.vector.tensor_scalar(rs, K.ps[:, 4, :], 1.0 / RET_V, EPS, ALU.mult, ALU.add)\
                        .then_inc(S["var"], 1)
                    dve.wait_ge(S["std"], n + 1)
                    link(dve, nc.vector.reciprocal(rs, rs))
                    oh = o[:, h * NV:(h + 1) * NV, :]
                    nc.vector.tensor_tensor(oh, oh, rs.unsqueeze(1).to_broadcast([P, NV, SEQ]), ALU.mult)\
                        .then_inc(S["scaled"], 1)


def gate_and_project(K, w, o, y):
    nc = K.nc
    freed = K.outs_freed
    S = {n: K.sem(w.name + "_" + n) for n in ("silu", "product", "hi")}
    with ExitStack() as ctx:
        silu = K.sb(w.name + "_silu", [P, 2, SEQ], ctx=ctx)
        with nc.Block() as block:
            @block.sync
            def _(sp):
                K.over_tiles(sp, w, lambda i, last: K.loads(sp, w, i, last))

            @block.scalar
            def _(act):
                def trip(i, last):
                    for j in range(w.unroll):
                        t = i * w.unroll + j
                        K.split_ahead(K.split_hi, act, w, i, j, last)
                        act.wait_ge(K.tile_used, K.tile_no(w, i, j) + 1)
                        act.wait_ge(K.psum_free, i * w.unroll + (freed + j))
                        nc.scalar.activation(silu[:], K.ps[:, (j % 2) * 2:(j % 2) * 2 + 2, :], ACT.Silu)\
                            .then_inc(S["silu"], 1)
                        act.wait_ge(S["product"], t + 1)
                        nc.scalar.activation(y[0][:, bass.ds(2 * t, 2), :], silu[:], ACT.Copy).then_inc(S["hi"], 1)
                K.over_tiles(act, w, trip)

            @block.vector
            def _(dve):
                def trip(i, last):
                    for j in range(w.unroll):
                        t = i * w.unroll + j
                        K.split_ahead(K.split_lo, dve, w, i, j, last)
                        dve.wait_ge(S["silu"], t + 1)
                        nc.vector.tensor_tensor(silu[:], silu[:], o[:, bass.ds(2 * t, 2), :], ALU.mult)\
                            .then_inc(S["product"], 1)
                        dve.wait_ge(S["hi"], t + 1)
                        nc.vector.tensor_tensor(y[1][:, bass.ds(2 * t, 2), :], silu[:],
                                                y[0][:, bass.ds(2 * t, 2), :].bitcast(F32), ALU.subtract)\
                            .then_inc(K.psum_free, 1)
                K.over_tiles(dve, w, trip)

            @block.tensor
            def _(pe):
                def trip(i, last):
                    for j in range(w.unroll):
                        pe.wait_ge(K.lo_ready, K.tile_no(w, i, j) + 1)
                        pe.wait_ge(K.psum_free, i * w.unroll + (freed + j - 1))
                        hi, lo = K.weights(w, j, K.w_hi), K.weights(w, j, K.w_lo)
                        for m in range(2):
                            for c in range(DC):
                                mm = split_products(
                                    nc, K.ps[:, (j % 2) * 2 + m, :], hi[:, c, m * P:(m + 1) * P],
                                    lo[:, c, m * P:(m + 1) * P], K.h_hi[:, c, N_META:T], K.h_lo[:, c, N_META:T],
                                    c == 0, c == DC - 1)
                        mm.then_inc(K.tile_used, 1)
                K.over_tiles(pe, w, trip)
    K.outs_freed += w.tiles


def modulations(K, I, W, layer):
    nc = K.nc
    MC = 6 * DC
    mod = [K.sb("mod%d" % n, [P, MC], ctx=layer) for n in range(2)]
    gains = K.sb("mod_gains", [P, 4, DC], ctx=layer)
    K.conv_cols = K.sb("gdn_conv_cols", [P, 4 * GDN_CH], ctx=layer)
    S = {n: K.sem("mod_" + n) for n in ("loaded", "turned", "read", "silu", "hi", "cond")}
    with ExitStack() as ctx:
        b_cols = K.sb("b_ada_cols", [P, 2 * MC], ctx=ctx)
        rows = K.sb("mod_rows", [P, 2, P], ctx=ctx)
        cond = K.sb("cond", [P, DC], ctx=ctx)
        c_hi = K.sb("cond_hi", [P, DC, 2], F32R, ctx)
        c_lo = K.sb("cond_lo", [P, DC, 2], F32R, ctx)
        with nc.Block() as block:
            @block.sync
            def _(sp):
                load_all(K, sp, [
                    (rows[0:2 * MC, 0, :], I["b_ada_2"].rearrange("l (c p) -> (l c) p", p=P)),
                    (rows[0:4 * GDN_CH, 1, :], I["gdn_conv_2"].rearrange("a j (c p) -> (a j c) p", p=P))], S["loaded"])

            @block.tensor
            def _(pe):
                pe.wait_ge(S["loaded"], 32)
                for n in range(2):
                    nc.tensor.transpose(K.ps[:, n, 0:2 * MC], rows[0:2 * MC, n, :], K.ident[0:2 * MC, 0:2 * MC])\
                        .then_inc(S["turned"], 1)

            @block.scalar
            def _(act):
                nc.scalar.activation(cond[:], param(K, "cond", DC), ACT.Silu).then_inc(S["silu"], 1)
                act.wait_ge(S["silu"], 1)
                nc.scalar.activation(c_hi[:], cond[:].unsqueeze(2).to_broadcast([P, DC, 2]), ACT.Copy)\
                    .then_inc(S["hi"], 1)
                for n, dst in enumerate((b_cols, K.conv_cols)):
                    act.wait_ge(S["turned"], n + 1)
                    nc.scalar.activation(dst[:], K.ps[:, n, 0:2 * MC], ACT.Copy)

            @block.vector
            def _(dve):
                dve.wait_ge(S["hi"], 1)
                nc.vector.tensor_tensor(c_lo[:], cond[:].unsqueeze(2).to_broadcast([P, DC, 2]),
                                        c_hi[:].bitcast(F32), ALU.subtract)
        for n in range(2):
            project_column(K, W["ada_%d" % n], c_hi, c_lo, b_cols[:, n * MC:(n + 1) * MC], mod[n])
        with nc.Block() as block:
            @block.vector
            def _(dve):
                for n in range(2):
                    for m, (name, at) in enumerate((("norm_mix_2", 1), ("norm_ffn_2", 4))):
                        nc.vector.scalar_tensor_tensor(gains[:, 2 * n + m, :], mod[n][:, at * DC:(at + 1) * DC], 1.0,
                                                       param(K, name, 2 * DC)[:, n * DC:(n + 1) * DC],
                                                       ALU.add, ALU.mult)

    def part(n, at):
        return mod[n][:, at * DC:(at + 1) * DC]
    return [[(gains[:, 2 * n + m, :], part(n, 3 * m), part(n, 3 * m + 2)) for m in range(2)] for n in range(2)]


def project_column(K, w, v_hi, v_lo, bias, dest):
    nc = K.nc
    freed = K.outs_freed
    with nc.Block() as block:
        @block.sync
        def _(sp):
            K.over_tiles(sp, w, lambda i, last: K.loads(sp, w, i, last))

        @block.scalar
        def _(act):
            def trip(i, last):
                for j in range(w.unroll):
                    K.split_ahead(K.split_hi, act, w, i, j, last)
            K.over_tiles(act, w, trip)

        @block.vector
        def _(dve):
            def trip(i, last):
                for j in range(w.unroll):
                    K.split_ahead(K.split_lo, dve, w, i, j, last)
                    dve.wait_ge(K.tile_used, K.tile_no(w, i, j) + 1)
                    at = bass.ds(i * (2 * w.unroll) + 2 * j, 2)
                    sums = K.ps[:, j % 2, 0:4].rearrange("p (m two) -> p m two", two=2)[:, :, 0]
                    nc.vector.tensor_tensor(dest[:, at], sums, bias[:, at], ALU.add).then_inc(K.psum_free, 1)
            K.over_tiles(dve, w, trip)

        @block.tensor
        def _(pe):
            def trip(i, last):
                for j in range(w.unroll):
                    pe.wait_ge(K.lo_ready, K.tile_no(w, i, j) + 1)
                    pe.wait_ge(K.psum_free, i * w.unroll + (freed + j - 1))
                    hi, lo = K.weights(w, j, K.w_hi), K.weights(w, j, K.w_lo)
                    for m in range(2):
                        for k in range(w.rows):
                            mm = split_products(nc, K.ps[:, j % 2, 2 * m:2 * m + 2], hi[:, k, m * P:(m + 1) * P],
                                                lo[:, k, m * P:(m + 1) * P], v_hi[:, k, :], v_lo[:, k, :],
                                                k == 0, k == w.rows - 1)
                    mm.then_inc(K.tile_used, 1)
            K.over_tiles(pe, w, trip)
    K.outs_freed += w.tiles


def project_conv(K, w, dest):
    nc = K.nc
    freed = K.outs_freed
    S = {n: K.sem("conv_" + n) for n in ("cleared", "copied", "tap", "silu")}
    PAD = 3
    with ExitStack() as ctx:
        pre = K.sb("conv_in", [P, 2, 2, PAD + SEQ], ctx=ctx)
        mixed = K.sb("conv_mixed", [P, 2, 2, SEQ], ctx=ctx)
        with nc.Block() as block:
            @block.gpsimd
            def _(pool):
                nc.gpsimd.memset(pre[:, :, :, 0:PAD], 0.0).then_inc(S["cleared"], 1)
        with nc.Block() as block:
            @block.sync
            def _(sp):
                K.over_tiles(sp, w, lambda i, last: K.loads(sp, w, i, last))

            @block.scalar
            def _(act):
                def trip(i, last):
                    for j in range(w.unroll):
                        t = i * w.unroll + j
                        K.split_ahead(K.split_hi, act, w, i, j, last)
                        act.wait_ge(K.tile_used, K.tile_no(w, i, j) + 1)
                        nc.scalar.activation(pre[:, j % 2, :, PAD:], K.ps[:, (j % 2) * 2:(j % 2) * 2 + 2, :],
                                             ACT.Copy).then_inc(S["copied"], 1)
                        act.wait_ge(S["tap"], 8 * t + 8)
                        nc.scalar.activation(dest[:, bass.ds(2 * t, 2), :], mixed[:, j % 2, :, :], ACT.Silu)\
                            .then_inc(K.psum_free, 1)
                K.over_tiles(act, w, trip)

            @block.vector
            def _(dve):
                def trip(i, last):
                    for j in range(w.unroll):
                        t = i * w.unroll + j
                        K.split_ahead(K.split_lo, dve, w, i, j, last)
                        dve.wait_ge(S["copied"], t + 1)
                        dve.wait_ge(K.psum_free, i * w.unroll + (freed + j - 1))
                        for tap in (3, 2, 1, 0):
                            for m in range(2):
                                by = K.conv_cols[:, bass.ds(2 * t + (tap * GDN_CH + m), 1)]
                                src, dst = pre[:, j % 2, m, tap:tap + SEQ], mixed[:, j % 2, m, :]
                                n = 2 * (3 - tap) + m
                                if tap == 3:
                                    ins = nc.vector.tensor_scalar(dst, src, by, None, ALU.mult)
                                else:
                                    dve.wait_ge(S["tap"], 8 * t + n - 1)
                                    ins = nc.vector.scalar_tensor_tensor(dst, src, by, dst, ALU.mult, ALU.add)
                                ins.then_inc(S["tap"], 1)
                K.over_tiles(dve, w, trip)

            @block.tensor
            def _(pe):
                def trip(i, last):
                    for j in range(w.unroll):
                        pe.wait_ge(K.lo_ready, K.tile_no(w, i, j) + 1)
                        pe.wait_ge(K.psum_free, i * w.unroll + (freed + j - 1))
                        hi, lo = K.weights(w, j, K.w_hi), K.weights(w, j, K.w_lo)
                        for m in range(2):
                            for c in range(DC):
                                mm = split_products(
                                    nc, K.ps[:, (j % 2) * 2 + m, :], hi[:, c, m * P:(m + 1) * P],
                                    lo[:, c, m * P:(m + 1) * P], K.h_hi[:, c, N_META:T], K.h_lo[:, c, N_META:T],
                                    c == 0, c == DC - 1)
                        mm.then_inc(K.tile_used, 1)
                K.over_tiles(pe, w, trip)
    K.outs_freed += w.tiles


def delta_rule(K, I, W, mods):
    nc = K.nc
    H = GDN_HEADS
    gain, shift, gate = mods
    with ExitStack() as layer:
        qkv = K.sb("gdn_qkv", [P, GDN_CH, SEQ], ctx=layer)
        z = K.sb("gdn_z", [P, H, SEQ], ctx=layer)
        rows = K.sb("gdn_rows", [2 * H, 2, SEQ], ctx=layer)
        with ExitStack() as proj:
            K.take_h("gdn_h", proj)
            normalize(K, ONLY_X, gain, shift)
            project_conv(K, W["gdn_qkv"], qkv)
            ab = K.sb("gdn_ab", [P, 1, SEQ], ctx=proj)
            project(K, W["gdn_ab"], ab, ONLY_X, base=N_META)
            delta_gates(K, I, ab, rows)
            project(K, W["gdn_z"], z, ONLY_X, base=N_META)
        with ExitStack() as core:
            delta_core(K, qkv, rows, core)
        o = qkv[:, 0:H, :]
        head_norm(K, "gdn_out", [(o[:, 4 * n:4 * n + 4, :], param(K, "out_norm", 1)) for n in range(2)],
                  K.ones[:], 1.0 / P)
        K.take_h("gdn_y", layer)
        S = {n: K.sem("gdn_y_" + n) for n in ("silu", "product", "hi")}
        with nc.Block() as block:
            @block.scalar
            def _(act):
                nc.scalar.activation(z[:], z[:], ACT.Silu).then_inc(S["silu"], 1)
                act.wait_ge(S["product"], 1)
                nc.scalar.activation(K.h_hi[:, :, N_META:T], z[:], ACT.Copy).then_inc(S["hi"], 1)

            @block.vector
            def _(dve):
                dve.wait_ge(S["silu"], 1)
                nc.vector.tensor_tensor(z[:], z[:], o, ALU.mult).then_inc(S["product"], 1)
                dve.wait_ge(S["hi"], 1)
                nc.vector.tensor_tensor(K.h_lo[:, :, N_META:T], z[:], K.h_hi[:, :, N_META:T].bitcast(F32), ALU.subtract)
        add_projected(K, W["gdn_out"], (K.h_hi, K.h_lo), ONLY_X, gate=gate)


def delta_gates(K, I, ab, rows):
    nc = K.nc
    H = GDN_HEADS
    S = {n: K.sem("gate_" + n) for n in ("loaded", "abs", "ez", "beta", "rate")}
    with ExitStack() as ctx:
        t = [K.sb("gate_t%d" % n, [H, SEQ], ctx=ctx) for n in range(4)]
        a_log = K.sb("gate_a_log", [H, 1], ctx=ctx)
        dt = K.sb("gate_dt", [H, 1], ctx=ctx)
        with nc.Block() as block:
            @block.sync
            def _(sp):
                load_all(K, sp, [(a_log[:], I["gdn_a_log_2"].rearrange("a h -> h a")),
                                 (dt[:], I["gdn_dt_bias_2"].rearrange("a h -> h a"))], S["loaded"])

            @block.scalar
            def _(act):
                act.wait_ge(S["loaded"], 32)
                nc.scalar.activation(t[0][:], ab[0:H, 0, :], ACT.Abs, bias=dt[:]).then_inc(S["abs"], 1)
                act.wait_ge(S["abs"], 1)
                nc.scalar.activation(t[0][:], t[0][:], ACT.Exp, scale=-1.0).then_inc(S["ez"], 1)
                nc.scalar.activation(a_log[:], a_log[:], ACT.Exp).then_inc(S["rate"], 1)
                nc.scalar.activation(rows[:, 1, :], ab[0:2 * H, 0, :], ACT.Sigmoid).then_inc(S["beta"], 1)

            @block.vector
            def _(dve):
                link = K.dve.link
                dve.wait_ge(S["ez"], 1)
                log1p_chain(K, dve, t[1][:], t[0][:], t[2][:], t[3][:])
                link(dve, nc.vector.tensor_scalar(t[2][:], ab[0:H, 0, :], dt[:], 0.0, ALU.add, ALU.max))
                link(dve, nc.vector.tensor_tensor(t[1][:], t[1][:], t[2][:], ALU.add))
                dve.wait_ge(S["rate"], 1)
                link(dve, nc.vector.tensor_scalar(t[1][:], t[1][:], a_log[:], -1.0, ALU.mult, ALU.mult))
                for c in range(QB):
                    at = slice(c * P, (c + 1) * P)
                    link(dve, nc.vector.tensor_tensor_scan(rows[0:H, 0, at], K.ones[0:H, :], t[1][:, at], 0.0,
                                                           ALU.mult, ALU.add))


def delta_core(K, qkv, rows, ctx):
    nc = K.nc
    H = GDN_HEADS
    LEVELS = 7
    head_norm(K, "gdn_unit", [(qkv[:, 4 * n:4 * n + 4, :], P ** -0.5 if n < 2 else 1.0) for n in range(4)],
              K.ones[:], 1.0)
    v_tok = K.sb("gdn_v_tok", [P, H, QB, P], ctx=ctx)
    a_t = K.sb("gdn_a_t", [P, H, QB, P], ctx=ctx)
    x_t = qkv[:, 2 * H:3 * H, :].rearrange("p h (c w) -> p h c w", c=QB)
    g_col = K.sb("gdn_g_col", [P, QB, H], ctx=ctx)
    b_col = K.sb("gdn_b_col", [P, QB, 2 * H], ctx=ctx)
    g_last = K.sb("gdn_g_last", [P, QB, H], ctx=ctx)
    e_beta = K.sb("gdn_e_beta", [P, QB, H], ctx=ctx)
    e_rest = K.sb("gdn_e_rest", [P, QB, H], ctx=ctx)
    select = K.sb("gdn_select", [2 * H, 2, H, P], ctx=ctx)
    causal = K.sb("gdn_causal", [P, P], ctx=ctx)
    levels = K.sb("gdn_levels", [P, LEVELS, P], ctx=ctx)
    S = {n: K.sem("gdn_" + n) for n in ("loaded", "turned", "kept", "cols", "last", "e")}

    def turn_heads(pe, first, sems):
        for n in range(H):
            if n >= 4:
                pe.wait_ge(sems["kept"], n - 3)
            for c in range(QB):
                mm = nc.tensor.transpose(K.ps[:, n % 4, c * P:(c + 1) * P],
                                         qkv[:, first + n, c * P:(c + 1) * P], K.ident[:])
            mm.then_inc(sems["turned"], 1)

    def keep_heads(act, dst, sems):
        for n in range(H):
            act.wait_ge(sems["turned"], n + 1)
            nc.scalar.activation(dst[:, n, :, :], K.ps[:, n % 4, :].rearrange("p (c w) -> p c w", c=QB), ACT.Copy)\
                .then_inc(sems["kept"], 1)

    with nc.Block() as block:
        @block.sync
        def _(sp):
            load_all(K, sp, [(select[:].rearrange("p a h w -> p (a h w)"), K.const["gdn_select"][:]),
                             (causal[:], K.const["gdn_causal"][:]),
                             (levels[:].rearrange("p l w -> p (l w)"), K.const["gdn_levels"][:])], S["loaded"])
            sp.wait_ge(S["loaded"], 48)

        @block.tensor
        def _(pe):
            turn_heads(pe, 2 * H, S)
            for c in range(QB):
                nc.tensor.transpose(K.ps[:, 4, c * H:(c + 1) * H], rows[0:H, 0, c * P:(c + 1) * P], K.ident[0:H, 0:H])
                mm = nc.tensor.transpose(K.ps[:, 5, c * 2 * H:(c + 1) * 2 * H], rows[:, 1, c * P:(c + 1) * P],
                                         K.ident[0:2 * H, 0:2 * H])
            mm.then_inc(S["cols"], 1)

        @block.scalar
        def _(act):
            keep_heads(act, v_tok, S)

        @block.vector
        def _(dve):
            dve.wait_ge(S["cols"], 1)
            nc.vector.tensor_copy(g_col[:], K.ps[:, 4, 0:QB * H].rearrange("p (c h) -> p c h", c=QB))
            nc.vector.tensor_copy(b_col[:], K.ps[:, 5, 0:QB * 2 * H].rearrange("p (c h) -> p c h", c=QB))

    D1 = {n: K.sem("x_" + n) for n in ("rows", "diff", "decay", "keys", "q_done", "a_done", "l_done", "cut",
                                       "turned", "x0", "x_kept", "y", "y_kept", "p", "x", "q_scaled")}
    with ExitStack() as inner:
        decay = K.sb("x_decay", [P, 2, QB, P], ctx=inner)
        lower = K.sb("x_lower", [P, 2, QB, P], ctx=inner)
        cut = K.sb("x_cut", [P, 2, QB, P], ctx=inner)
        x = K.sb("x_x", [P, 2, QB, P], ctx=inner)
        y = K.sb("x_y", [P, 2, QB, P], ctx=inner)
        e_row = K.sb("x_e_row", [P, 2, SEQ], ctx=inner)

        def bank(h, n):
            return K.ps[:, 4 * (h % 2) + n, :]

        def by_chunk(ap):
            return ap.rearrange("p (c w) -> p c w", c=QB)

        def at(c):
            return slice(c * P, (c + 1) * P)
        pairs = [(2 * n, 2 * n + 1) for n in range(H // 2)]
        with nc.Block() as block:
            @block.tensor
            def _(pe):
                for n, pair in enumerate(pairs):
                    for h in pair:
                        if n:
                            pe.wait_ge(D1["x"], (LEVELS - 1) * 2 * n)
                        nc.tensor.matmul(bank(h, 0), select[0:H, 0, h, :], rows[0:H, 0, :], start=True, stop=True)
                        nc.tensor.matmul(bank(h, 1), select[:, 1, h, :], rows[:, 1, :], start=True, stop=True)\
                            .then_inc(D1["rows"], 1)
                        for c in range(QB):
                            kc = qkv[:, H + h, at(c)]
                            nc.tensor.matmul(bank(h, 2)[:, at(c)], kc, kc, start=True, stop=True)
                            mm = nc.tensor.matmul(bank(h, 3)[:, at(c)], kc, qkv[:, h, at(c)], start=True, stop=True)
                        mm.then_inc(D1["keys"], 1)
                    for h in pair:
                        pe.wait_ge(D1["x0"], h + 1)
                        for c in range(QB):
                            mm = nc.tensor.transpose(bank(h, 3)[:, at(c)], x_t[:, h, c, :], K.ident[:])
                        mm.then_inc(D1["turned"], 1)
                    for level in range(1, LEVELS):
                        for h in pair:
                            done = (LEVELS - 1) * 2 * n + 2 * (level - 1) + h % 2
                            pe.wait_ge(D1["cut"], done + 1)
                            if level == 1:
                                pe.wait_ge(D1["x_kept"], h + 1)
                            else:
                                pe.wait_ge(D1["x"], done - 1)
                            for c in range(QB):
                                mm = nc.tensor.matmul(bank(h, 0)[:, at(c)], cut[:, h % 2, c, :], x[:, h % 2, c, :],
                                                      start=True, stop=True)
                            mm.then_inc(D1["y"], 1)
                        for h in pair:
                            done = (LEVELS - 1) * 2 * n + 2 * (level - 1) + h % 2
                            pe.wait_ge(D1["y_kept"], done + 1)
                            for c in range(QB):
                                nc.tensor.matmul(bank(h, 1)[:, at(c)], x_t[:, h, c, :], y[:, h % 2, c, :],
                                                 start=True, stop=True)
                            for c in range(QB):
                                mm = nc.tensor.matmul(bank(h, 2)[:, at(c)], y[:, h % 2, c, :], x_t[:, h, c, :],
                                                      start=True, stop=True)
                            mm.then_inc(D1["p"], 1)

            @block.scalar
            def _(act):
                for n, pair in enumerate(pairs):
                    for h in pair:
                        act.wait_ge(D1["rows"], h + 1)
                        act.wait_ge(D1["diff"], h + 1)
                        if h >= 2:
                            act.wait_ge(D1["q_scaled"], h - 1)
                        nc.scalar.activation(e_row[:, h % 2, :], bank(h, 0), ACT.Exp)
                        nc.scalar.activation(decay[:, h % 2, :, :], decay[:, h % 2, :, :], ACT.Exp)\
                            .then_inc(D1["decay"], 1)
                    for h in pair:
                        act.wait_ge(D1["turned"], h + 1)
                        nc.scalar.activation(x[:, h % 2, :, :], by_chunk(bank(h, 3)), ACT.Copy)\
                            .then_inc(D1["x_kept"], 1)
                    for level in range(1, LEVELS):
                        for h in pair:
                            done = (LEVELS - 1) * 2 * n + 2 * (level - 1) + h % 2
                            act.wait_ge(D1["y"], done + 1)
                            nc.scalar.activation(y[:, h % 2, :, :], by_chunk(bank(h, 0)), ACT.Copy)\
                                .then_inc(D1["y_kept"], 1)

            @block.vector
            def _(dve):
                link = K.dve.link
                wide = [P, QB, P]

                def level_mask(level):
                    return levels[:, level, :].unsqueeze(1).to_broadcast(wide)
                for n, pair in enumerate(pairs):
                    for h in pair:
                        dve.wait_ge(D1["rows"], h + 1)
                        d, low = decay[:, h % 2, :, :], lower[:, h % 2, :, :]
                        nc.vector.tensor_copy(g_last[:, :, h], by_chunk(bank(h, 0))[:, :, P - 1])
                        for c in range(QB):
                            ins = nc.vector.scalar_tensor_tensor(d[:, c, :], bank(h, 0)[:, at(c)], g_col[:, c, h:h + 1],
                                                                 causal[:], ALU.subtract, ALU.min)
                        ins.then_inc(D1["diff"], 1)
                    for h in pair:
                        d, low = decay[:, h % 2, :, :], lower[:, h % 2, :, :]
                        dve.wait_ge(D1["decay"], h + 1)
                        dve.wait_ge(D1["keys"], h + 1)
                        nc.vector.tensor_tensor(a_t[:, h, :, :], by_chunk(bank(h, 3)), d, ALU.mult)
                        link(dve, nc.vector.tensor_tensor(low, by_chunk(bank(h, 2)), d, ALU.mult))
                        link(dve, nc.vector.tensor_tensor(low, by_chunk(bank(h, 1)), low, ALU.mult))
                        link(dve, nc.vector.tensor_tensor(x_t[:, h, :, :], low, level_mask(0), ALU.mult))
                        nc.vector.tensor_tensor(x_t[:, h, :, :], K.ident[:].unsqueeze(1).to_broadcast(wide),
                                                x_t[:, h, :, :], ALU.subtract).then_inc(D1["x0"], 1)
                        nc.vector.tensor_tensor(qkv[:, h, :], qkv[:, h, :], e_row[:, h % 2, :], ALU.mult)\
                            .then_inc(D1["q_scaled"], 1)
                    for level in range(1, LEVELS):
                        for h in pair:
                            nc.vector.tensor_tensor(cut[:, h % 2, :, :], lower[:, h % 2, :, :], level_mask(level),
                                                    ALU.mult).then_inc(D1["cut"], 1)
                        for h in pair:
                            done = (LEVELS - 1) * 2 * n + 2 * (level - 1) + h % 2
                            dve.wait_ge(D1["p"], done + 1)
                            xs = x[:, h % 2, :, :]
                            if level < LEVELS - 1:
                                link(dve, nc.vector.tensor_tensor(xs, xs, by_chunk(bank(h, 1)), ALU.subtract))
                            nc.vector.tensor_tensor(x_t[:, h, :, :], x_t[:, h, :, :], by_chunk(bank(h, 2)),
                                                    ALU.subtract).then_inc(D1["x"], 1)

    R = {n: K.sem("rule_" + n) for n in ("e", "turned", "kept", "k_s", "rest", "v", "v_kept", "out", "out_kept", "state")}
    state = K.sb("rule_state", [P, H, P], ctx=ctx)
    rest = K.sb("rule_rest", [P, H, P], ctx=ctx)
    v_new = K.sb("rule_v", [P, H, P], ctx=ctx)
    e_last = K.sb("rule_e_last", [P, QB, H], ctx=ctx)

    def group(G, n):
        return K.ps[:, 4 * G + n, :].rearrange("p (h w) -> p h w", h=4)

    def wide(col, G, c):
        return col[:, c, 4 * G:4 * G + 4].unsqueeze(2).to_broadcast([P, 4, P])
    four = [slice(0, 4), slice(4, 8)]
    k_tok = K.sb("gdn_k_tok", [P, H, QB, P], ctx=ctx)
    with nc.Block() as block:
        @block.vector
        def _(dve):
            link = K.dve.link
            link(dve, nc.vector.tensor_tensor(e_rest[:], g_last[:], g_col[:], ALU.subtract))
            dve.wait_ge(R["e"], 1)
            nc.vector.tensor_tensor(e_beta[:], e_beta[:], b_col[:, :, H:2 * H], ALU.mult)
            for h in range(H):
                nc.vector.tensor_tensor(v_tok[:, h, :, :], v_tok[:, h, :, :],
                                        b_col[:, :, H + h].unsqueeze(2).to_broadcast([P, QB, P]), ALU.mult)

        @block.scalar
        def _(act):
            act.wait_ge(K.dve.sem, K.dve.n)
            nc.scalar.activation(e_rest[:], e_rest[:], ACT.Exp)
            nc.scalar.activation(e_last[:], g_last[:], ACT.Exp)
            nc.scalar.activation(e_beta[:], g_col[:], ACT.Exp).then_inc(R["e"], 1)
            keep_heads(act, k_tok, R)

        @block.tensor
        def _(pe):
            turn_heads(pe, H, R)

        @block.gpsimd
        def _(pool):
            pool.wait_ge(R["e"], 1)
            for h in range(H):
                pool.wait_ge(R["kept"], h + 1)
                nc.gpsimd.tensor_tensor(k_tok[:, h, :, :], k_tok[:, h, :, :],
                                        e_rest[:, :, h].unsqueeze(2).to_broadcast([P, QB, P]), ALU.mult)
    with nc.Block() as block:
        @block.tensor
        def _(pe):
            for c in range(QB):
                at = slice(c * P, (c + 1) * P)
                for G in range(2):
                    if c:
                        pe.wait_ge(R["state"], 2 * (c - 1) + G + 1)
                        for u in range(4):
                            h = 4 * G + u
                            mm = nc.tensor.matmul(group(G, 0)[:, u, :], qkv[:, H + h, at], state[:, h, :],
                                                  start=True, stop=True)
                        mm.then_inc(R["k_s"], 1)
                for G in range(2):
                    if c:
                        pe.wait_ge(R["rest"], 2 * (c - 1) + G + 1)
                    for u in range(4):
                        h = 4 * G + u
                        mm = nc.tensor.matmul(group(G, 1)[:, u, :], x_t[:, h, c, :],
                                              rest[:, h, :] if c else v_tok[:, h, 0, :], start=True, stop=True)
                    mm.then_inc(R["v"], 1)
                for G in range(2):
                    pe.wait_ge(R["v_kept"], 2 * c + G + 1)
                    if c:
                        pe.wait_ge(R["out_kept"], 2 * (c - 1) + G + 1)
                    for u in range(4):
                        h = 4 * G + u
                        if c:
                            nc.tensor.matmul(group(G, 2)[:, u, :], state[:, h, :], qkv[:, h, at], start=True, stop=False)
                        mm = nc.tensor.matmul(group(G, 2)[:, u, :], v_new[:, h, :], a_t[:, h, c, :],
                                              start=c == 0, stop=True)
                        if c < QB - 1:
                            mm = nc.tensor.matmul(group(G, 3)[:, u, :], k_tok[:, h, c, :], v_new[:, h, :],
                                                  start=True, stop=True)
                    mm.then_inc(R["out"], 1)

        @block.scalar
        def _(act):
            for c in range(QB):
                for G in range(2):
                    act.wait_ge(R["v"], 2 * c + G + 1)
                    nc.scalar.activation(v_new[:, four[G], :], group(G, 1), ACT.Copy).then_inc(R["v_kept"], 1)
                for G in range(2):
                    act.wait_ge(R["out"], 2 * c + G + 1)
                    nc.scalar.activation(qkv[:, four[G], c * P:(c + 1) * P], group(G, 2), ACT.Copy)\
                        .then_inc(R["out_kept"], 1)

        @block.vector
        def _(dve):
            link = K.dve.link
            for c in range(QB):
                for G in range(2):
                    if c:
                        dve.wait_ge(R["k_s"], 2 * (c - 1) + G + 1)
                        link(dve, nc.vector.tensor_tensor(rest[:, four[G], :], group(G, 0), wide(e_beta, G, c), ALU.mult))
                        nc.vector.tensor_tensor(rest[:, four[G], :], v_tok[:, four[G], c, :], rest[:, four[G], :],
                                                ALU.subtract).then_inc(R["rest"], 1)
                if c == QB - 1:
                    continue
                for G in range(2):
                    dve.wait_ge(R["out"], 2 * c + G + 1)
                    st = state[:, four[G], :]
                    if c == 0:
                        nc.vector.tensor_copy(st, group(G, 3)).then_inc(R["state"], 1)
                    else:
                        link(dve, nc.vector.tensor_tensor(st, st, wide(e_last, G, c), ALU.mult))
                        nc.vector.tensor_tensor(st, st, group(G, 3), ALU.add).then_inc(R["state"], 1)


def gate_weights(name, matrix):
    rowwise = matrix.rearrange("(k p) c -> p k c", p=P)
    n = 2 * GDN_HEADS
    last = matrix.shape[1] - n

    def source(i, j):
        def part(a, b):
            return lambda slot: slot.rearrange("p (k c) -> p k c", k=DC)[:, :, a:b]
        return [(part(0, n), rowwise[:, :, last:last + n]), (part(n, P), rowwise[:, :, 0:P - n])]
    w = Weights(name, 1, 1, (DC, P), source)
    w.loads = 2
    return w


def token_order(group):
    dilated = DSW_GROUPS[group][1] > 1

    def tile(ap, b):
        return ap.rearrange("p (i r) -> p r i", r=QB)[:, b, :] if dilated else ap[:, b * P:(b + 1) * P]
    return tile


def bias_windows():
    return [(2 * P, P, 1, 1), (P, 0, QB, 1), (P, 0, QB, DSW_GROUPS[2][1] // QB)]


def dilated_attention(K, I, W, mods):
    nc = K.nc
    H = DSW_HEADS
    gain, shift, gate = mods
    with ExitStack() as layer:
        qk = K.sb("dsw_qk_t", [P, 24, SEQ], ctx=layer)
        v = [K.sb("dsw_v%d_t" % g, [P, QB, H * HD], ctx=layer) for g in range(3)]
        with ExitStack() as proj:
            K.take_h("dsw_h", proj)
            normalize(K, ONLY_X, gain, shift)
            project(K, W["dsw_qk"], qk, ONLY_X, base=N_META)
            for g in range(3):
                tile = token_order(g)
                views = [(lambda h, k, b=b, tile=tile: tile(h[:, k, N_META:T], b), P) for b in range(QB)]
                project_tokens(K, W["dsw_v%d" % g], views,
                               lambda b, i, j, g=g: v[g][:, b, j * 256:(j + 1) * 256])
        y = K.sb("dsw_y", [P, ATT_CH, SEQ], ctx=layer)
        with ExitStack() as core:
            dilated_core(K, I, qk, v, y, core)
        y_hi = K.sb("dsw_y_hi", [P, ATT_CH, SEQ], F32R, layer)
        y_lo = K.sb("dsw_y_lo", [P, ATT_CH, SEQ], F32R, layer)
        kept = K.sem("dsw_y_kept")
        with nc.Block() as block:
            @block.scalar
            def _(act):
                nc.scalar.activation(y_hi[:], y[:], ACT.Copy).then_inc(kept, 1)

            @block.vector
            def _(dve):
                dve.wait_ge(kept, 1)
                nc.vector.tensor_tensor(y_lo[:], y[:], y_hi[:].bitcast(F32), ALU.subtract)
        add_projected(K, W["dsw_out"], (y_hi, y_lo), ONLY_X, base=N_META, gate=gate)


def dilated_core(K, I, qk, v, y, ctx):
    nc = K.nc
    H = DSW_HEADS
    NG = len(DSW_GROUPS)
    head_ones = K.sb("dsw_head_ones", [P, P], ctx=ctx)
    keys = [w[0] for w in bias_windows()]
    bias = [K.sb("dsw_bias%d" % g, [P, H, keys[g]], ctx=ctx) for g in range(NG)]
    spread = K.sb("dsw_spread", [H, ATT_CH, P], ctx=ctx)
    B = {n: K.sem("bias_" + n) for n in ("loaded", "ones", "rows", "kept", "written", "read")}
    q_gain = K.sb("dsw_q_gain", [P, 1], ctx=ctx)
    lengths = [P + w[0] - 1 for w in bias_windows()]
    starts = [sum(lengths[:g]) for g in range(NG)]
    total_len = sum(lengths)
    scratch = [nc.dram_tensor("bias_rows%d" % g, [H, P, lengths[g]], F32, kind="Internal").ap() for g in range(NG)]
    with ExitStack() as inner:
        pick = K.sb("bias_pick", [REL_BUCKETS + 1, total_len], ctx=inner)
        table = K.sb("bias_table", [REL_BUCKETS + 1, NG * H], ctx=inner)
        by_distance = K.sb("bias_by_distance", [H, total_len], ctx=inner)
        with nc.Block() as block:
            @block.gpsimd
            def _(pool):
                nc.gpsimd.memset(table[:], 1.0).then_inc(B["ones"], 1)

            @block.sync
            def _(sp):
                load_all(K, sp, [(pick[:], K.const["dsw_pick"][:]), (head_ones[:], K.const["head_ones"][:]),
                                 (spread[:].rearrange("h c w -> h (c w)"), K.const["dsw_spread"][:])], B["loaded"])
                sp.wait_ge(B["ones"], 1)
                sp.dma_start(table[0:REL_BUCKETS, :], I["rel_bias_2"]).then_inc(B["loaded"], 16)
                sp.wait_ge(B["kept"], NG)
                for g in range(NG):
                    src = by_distance[:, starts[g]:starts[g] + lengths[g]]
                    sp.dma_start(scratch[g], src.unsqueeze(1).to_broadcast([H, P, lengths[g]]))\
                        .then_inc(B["written"], 16)
                sp.wait_ge(B["written"], 16 * NG)
                for g in range(NG):
                    src = bass.AP(scratch[g].tensor, P - 1, [[lengths[g] - 1, P], [P * lengths[g], H], [1, keys[g]]])
                    sp.dma_start(bias[g][:], src).then_inc(B["read"], 16)
                sp.wait_ge(B["read"], 16 * NG)

            @block.tensor
            def _(pe):
                pe.wait_ge(B["loaded"], 64)
                for g in range(NG):
                    nc.tensor.matmul(K.ps[0:H, g, 0:lengths[g]], table[:, g * H:(g + 1) * H],
                                     pick[:, starts[g]:starts[g] + lengths[g]], start=True, stop=True)\
                        .then_inc(B["rows"], 1)

            @block.vector
            def _(dve):
                nc.vector.tensor_scalar(q_gain[:], param(K, "dsw_q_norm", 1), HD ** -0.5, None, ALU.mult)
                for g in range(NG):
                    dve.wait_ge(B["rows"], g + 1)
                    nc.vector.tensor_copy(by_distance[:, starts[g]:starts[g] + lengths[g]],
                                          K.ps[0:H, g, 0:lengths[g]]).then_inc(B["kept"], 1)
    parts = [(qk[:, 4 * n:4 * n + 4, :], q_gain[:] if n < 3 else param(K, "dsw_k_norm", 1)) for n in range(6)]
    head_norm(K, "dsw_norm", parts, head_ones[:], 1.0 / HD)

    outs = K.sb("dsw_outs", [P, NG, ATT_CH, SEQ], ctx=ctx)
    tops = K.sb("dsw_tops", [P, NG, QB, H], ctx=ctx)
    sums = K.sb("dsw_sums", [P, NG, QB, H], ctx=ctx)
    S = {n: K.sem("dsw_" + n) for n in ("scores", "biased", "max", "exp", "turned", "turned_read", "out", "kept")}
    steps = [(g, b, quad) for g in range(NG) for b in range(QB) for quad in range(2)]
    with ExitStack() as inner:
        s = K.sb("dsw_s", [P, 2, 4, 2 * P], ctx=inner)
        pt = K.sb("dsw_pt", [P, 2, 2 * P], ctx=inner)
        minus = K.sb("dsw_minus", [P, 2, 4], ctx=inner)

        def key_tiles(g, b):
            return [b - 1, b] if g == 0 and b else [b]

        with nc.Block() as block:
            @block.tensor
            def _(pe):
                def scores(n):
                    g, b, quad = steps[n]
                    tile = token_order(g)
                    if n >= 1:
                        pe.wait_ge(S["biased"], n)
                    for u in range(4):
                        half = slice((u % 2) * HD, (u % 2 + 1) * HD)
                        chunk = 4 * g + 2 * quad + u // 2
                        query = tile(qk[half, chunk, :], b)
                        for m, kb in enumerate(key_tiles(g, b)):
                            mm = nc.tensor.matmul(K.ps[:, u, m * P:(m + 1) * P], query,
                                                  tile(qk[half, 12 + chunk, :], kb), start=True, stop=True)
                    mm.then_inc(S["scores"], 1)
                scores(0)
                for n, (g, b, quad) in enumerate(steps):
                    if n + 1 < len(steps):
                        scores(n + 1)
                    pe.wait_ge(S["exp"], n + 1)
                    if n >= 2:
                        pe.wait_ge(S["kept"], n - 1)
                    tiles = key_tiles(g, b)

                    def turn(u):
                        e = 4 * n + u
                        if e >= 2:
                            pe.wait_ge(S["turned_read"], e - 1)
                        for m in range(len(tiles)):
                            mm = nc.tensor.transpose(K.ps[:, 4 + u % 2, m * P:(m + 1) * P],
                                                     s[:, n % 2, u, m * P:(m + 1) * P], K.ident[:])
                        mm.then_inc(S["turned"], 1)
                    turn(0)
                    for u in range(4):
                        if u < 3:
                            turn(u + 1)
                        pe.wait_ge(S["turned_read"], 4 * n + u + 1)
                        out = K.ps[(u % 2) * HD:(u % 2 + 1) * HD, 6 + n % 2, (u // 2) * P:(u // 2 + 1) * P]
                        h = 4 * quad + u
                        for m, kb in enumerate(tiles):
                            mm = nc.tensor.matmul(out, v[g][:, kb, h * HD:(h + 1) * HD],
                                                  pt[:, u % 2, m * P:(m + 1) * P], start=m == 0,
                                                  stop=m == len(tiles) - 1)
                    mm.then_inc(S["out"], 1)

            @block.vector
            def _(dve):
                link = K.dve.link
                for n, (g, b, quad) in enumerate(steps):
                    nk = P * len(key_tiles(g, b))
                    sv = s[:, n % 2, :, 0:nk]
                    heads = slice(4 * quad, 4 * quad + 4)
                    dve.wait_ge(S["scores"], n + 1)
                    if n >= 2:
                        dve.wait_ge(S["turned"], 4 * (n - 1))
                    nc.vector.tensor_tensor(sv, K.ps[:, 0:4, 0:nk], bias[g][:, heads, keys[g] - nk:keys[g]], ALU.add)\
                        .then_inc(S["biased"], 1)
                    dve.wait_ge(S["biased"], n + 1)
                    top = tops[:, g, b, heads]
                    link(dve, nc.vector.tensor_reduce(top, sv, AX_X, ALU.max))
                    nc.vector.tensor_scalar(minus[:, n % 2, :], top, -1.0, None, ALU.mult).then_inc(S["max"], 1)

            @block.scalar
            def _(act):
                def exps(n):
                    g, b, quad = steps[n]
                    nk = P * len(key_tiles(g, b))
                    act.wait_ge(S["max"], n + 1)
                    for u in range(4):
                        h = 4 * quad + u
                        ins = nc.scalar.activation(s[:, n % 2, u, 0:nk], s[:, n % 2, u, 0:nk], ACT.Exp,
                                                   bias=minus[:, n % 2, u:u + 1], accum_out=sums[:, g, b, h:h + 1])
                    ins.then_inc(S["exp"], 1)
                exps(0)
                for n, (g, b, quad) in enumerate(steps):
                    nk = P * len(key_tiles(g, b))
                    for u in range(4):
                        act.wait_ge(S["turned"], 4 * n + u + 1)
                        nc.scalar.activation(pt[:, u % 2, 0:nk], K.ps[:, 4 + u % 2, 0:nk], ACT.Copy)\
                            .then_inc(S["turned_read"], 1)
                    if n + 1 < len(steps):
                        exps(n + 1)
                    act.wait_ge(S["out"], n + 1)
                    for m in range(2):
                        dst = token_order(g)(outs[:, g, 2 * quad + m, :], b)
                        src = K.ps[:, 6 + n % 2, m * P:(m + 1) * P]
                        ins = nc.scalar.activation(dst, src, ACT.Copy)
                    ins.then_inc(S["kept"], 1)

    M = {n: K.sem("mix_" + n) for n in ("turned", "kept", "shifted", "e", "weights", "spread", "read")}
    with ExitStack() as inner:
        m_row = K.sb("mix_m", [H, NG, SEQ], ctx=inner)
        l_row = K.sb("mix_l", [H, NG, SEQ], ctx=inner)
        t_row = K.sb("mix_t", [H, SEQ], ctx=inner)
        z_row = K.sb("mix_z", [H, SEQ], ctx=inner)
        with nc.Block() as block:
            @block.tensor
            def _(pe):
                for n, src in enumerate((tops, sums)):
                    for g in range(NG):
                        for b in range(QB):
                            mm = nc.tensor.transpose(K.ps[0:H, 3 * n + g, b * P:(b + 1) * P], src[:, g, b, :], K.ident[:])
                        mm.then_inc(M["turned"], 1)
                pe.wait_ge(M["kept"], 2 * NG)
                pe.wait_ge(M["weights"], 1)
                for c in range(ATT_CH):
                    for g in range(NG):
                        n = c * NG + g
                        if n >= 4:
                            pe.wait_ge(M["read"], n - 3)
                        nc.tensor.matmul(K.ps[:, n % 4, :], spread[:, c, :], m_row[:, g, :], start=True, stop=True)\
                            .then_inc(M["spread"], 1)

            @block.scalar
            def _(act):
                for n, dst in enumerate((m_row, l_row)):
                    for g in range(NG):
                        act.wait_ge(M["turned"], 3 * n + g + 1)
                        for b in range(QB):
                            src = K.ps[0:H, 3 * n + g, b * P:(b + 1) * P]
                            ins = nc.scalar.activation(token_order(g)(dst[:, g, :], b), src, ACT.Copy)
                        ins.then_inc(M["kept"], 1)
                act.wait_ge(M["shifted"], 1)
                nc.scalar.activation(m_row[:], m_row[:], ACT.Exp).then_inc(M["e"], 1)

            @block.vector
            def _(dve):
                link = K.dve.link
                dve.wait_ge(M["kept"], 2 * NG)
                link(dve, nc.vector.tensor_tensor(t_row[:], m_row[:, 0, :], m_row[:, 1, :], ALU.max))
                link(dve, nc.vector.tensor_tensor(t_row[:], t_row[:], m_row[:, 2, :], ALU.max))
                nc.vector.tensor_tensor(m_row[:], m_row[:], t_row[:].unsqueeze(1).to_broadcast([H, NG, SEQ]),
                                        ALU.subtract).then_inc(M["shifted"], 1)
                dve.wait_ge(M["e"], 1)
                link(dve, nc.vector.tensor_tensor(l_row[:], l_row[:], m_row[:], ALU.mult))
                link(dve, nc.vector.tensor_tensor(z_row[:], l_row[:, 0, :], l_row[:, 1, :], ALU.add))
                link(dve, nc.vector.tensor_tensor(z_row[:], z_row[:], l_row[:, 2, :], ALU.add))
                link(dve, nc.vector.reciprocal(z_row[:], z_row[:]))
                nc.vector.tensor_tensor(m_row[:], m_row[:], z_row[:].unsqueeze(1).to_broadcast([H, NG, SEQ]), ALU.mult)\
                    .then_inc(M["weights"], 1)
                for c in range(ATT_CH):
                    for g in range(NG):
                        n = c * NG + g
                        dve.wait_ge(M["spread"], n + 1)
                        dst = y[:, c, :] if g == 0 else outs[:, g, c, :]
                        nc.vector.tensor_tensor(dst, K.ps[:, n % 4, :], outs[:, g, c, :], ALU.mult).then_inc(M["read"], 1)
                        if g:
                            dve.wait_ge(M["read"], n + 1)
                            link(dve, nc.vector.tensor_tensor(y[:, c, :], y[:, c, :], outs[:, g, c, :], ALU.add))


def two_blocks(nc, I, const, out):
    with ExitStack() as ctx:
        K = Core(nc, ctx)
        K.const = const
        ab = I["ab_w_in"].rearrange("a d n -> (a d) n")
        ret = I["ret_w_in"].rearrange("a d n -> (a d) n")
        W = {}
        W["ab_in"] = column_weights("ab_in", ab, 6, 2)
        W["ab_k"] = column_weights("ab_k", ab, 1, 1, P, first=1536)
        W["ab_v"] = column_weights("ab_v", ab, 1, 1, P, first=1664)
        W["ab_out"] = column_weights("ab_out", I["ab_w_out"][0], 4, 2)
        W["up_0"], W["down_0"] = up_weights("up_0", I["ffn_w_gu"][0]), down_weights("down_0", I["ffn_w_down"][0])
        W["ret_q"] = column_weights("ret_q", ret, 4, 2)
        W["ret_k"] = column_weights("ret_k", ret, 4, 2, first=D)
        W["ret_v0"] = column_weights("ret_v0", ret, 4, 2, first=2 * D)
        W["ret_v1"] = column_weights("ret_v1", ret, 4, 2, first=3 * D)
        W["ret_g"] = column_weights("ret_g", ret, 8, 2, first=4 * D)
        W["ret_out"] = column_weights("ret_out", I["ret_w_out"][0], 8, 2, P)
        W["up_1"], W["down_1"] = up_weights("up_1", I["ffn_w_gu"][1]), down_weights("down_1", I["ffn_w_down"][1])
        for n in range(2):
            W["ada_%d" % n] = column_weights("ada_%d" % n, I["w_ada_2"][n], 24, 2)
        gdn = I["gdn_w_in_2"].rearrange("a d n -> (a d) n")
        W["gdn_qkv"] = column_weights("gdn_qkv", gdn, 12, 2)
        W["gdn_ab"] = gate_weights("gdn_ab", gdn)
        W["gdn_z"] = column_weights("gdn_z", gdn, 4, 2, first=3 * D)
        W["gdn_out"] = column_weights("gdn_out", I["gdn_w_out_2"][0], 4, 2)
        W["up_2"], W["down_2"] = up_weights("up_2", I["w_ffn_in_2"][0]), down_weights("down_2", I["w_ffn_out_2"][0])
        dsw = I["dsw_w_in_2"].rearrange("a d n -> (a d) n")
        W["dsw_qk"] = column_weights("dsw_qk", dsw, 12, 2)
        for g in range(3):
            W["dsw_v%d" % g] = column_weights("dsw_v%d" % g, dsw, 2, 2, first=3072 + g * 512)
        W["dsw_out"] = column_weights("dsw_out", I["dsw_w_out_2"][0], 2, 2, 512)
        W["up_3"], W["down_3"] = up_weights("up_3", I["w_ffn_in_2"][1]), down_weights("down_3", I["w_ffn_out_2"][1])
        K.plan(list(W.values()))

        prologue(K, I, list(W.values())[0])
        with ExitStack() as layer:
            K.take_h("ab_h", layer)
            normalize(K, ALL, param(K, "norm_ab", 8))
            proj = K.sb("ab_proj", [P, 12, T], ctx=layer)
            key = K.sb("ab_key", [P, 1, T], ctx=layer)
            val = K.sb("ab_val", [P, QB, P], ctx=layer)
            val_meta = K.sb("ab_val_meta", [N_META, P], ctx=layer)
            project(K, W["ab_in"], proj, ALL)
            project(K, W["ab_k"], key, ALL)
            project_tokens(K, W["ab_v"], *token_blocks(val, val_meta, P))
            rg_lru(K, I, proj)
            window_attention(K, I, proj[:, 8:12, :], key[:], val[:], val_meta[:])
            add_projected(K, W["ab_out"], (K.h_hi, K.h_lo), ALL)
        K.end_layer()
        with ExitStack() as layer:
            K.take_h("ffn0_h", layer)
            normalize(K, ALL, param(K, "norm_ffn", 16)[:, 0:8])
            feed_forward(K, W["up_0"], W["down_0"], ALL)
        retention(K, W)
        K.end_layer()
        with ExitStack() as layer:
            K.take_h("ffn1_h", layer)
            normalize(K, ONLY_X, param(K, "norm_ffn", 16)[:, 8:16])
            feed_forward(K, W["up_1"], W["down_1"], ONLY_X)
        mods = modulations(K, I, W, ctx)
        delta_rule(K, I, W, mods[0][0])
        K.end_layer()
        modulated_feed_forward(K, W["up_2"], W["down_2"], mods[0][1])
        dilated_attention(K, I, W, mods[1][0])
        K.end_layer()
        modulated_feed_forward(K, W["up_3"], W["down_3"], mods[1][1])
        store(K, out)


def modulated_feed_forward(K, up, down, mods):
    gain, shift, gate = mods
    with ExitStack() as layer:
        K.take_h(up.name + "_h", layer)
        normalize(K, ONLY_X, gain, shift)
        feed_forward(K, up, down, ONLY_X, gate)


def token_blocks(val, val_meta, cols):
    views = [(lambda h, k, b=b: h[:, k, N_META + b * P:N_META + (b + 1) * P], P) for b in range(QB)]
    views.append((lambda h, k: h[:, k, 0:P], N_META))

    def dest(b, i, j):
        at = j * cols + i * (2 * cols)
        if b == QB:
            return val_meta[:, bass.ds(at, cols)]
        return val[:, b, bass.ds(at, cols)]
    return views, dest


def store(K, out):
    nc = K.nc
    turned, copied, stored = K.sem("end_turned"), K.sem("end_copied"), K.sem("end_stored")
    with ExitStack() as ctx:
        tok = K.sb("out_tokens", [P, QB, D], ctx=ctx)
        with nc.Block() as block:
            @block.tensor
            def _(pe):
                for b in range(QB):
                    for c in range(DC):
                        mm = nc.tensor.transpose(K.ps[:, 2 * b + c // 4, (c % 4) * P:(c % 4 + 1) * P],
                                                 K.x[:, c, N_META + b * P:N_META + (b + 1) * P], K.ident[:])
                    mm.then_inc(turned, 1)

            @block.scalar
            def _(act):
                for b in range(QB):
                    act.wait_ge(turned, b + 1)
                    nc.scalar.activation(tok[:, b, :], K.ps[:, 2 * b:2 * b + 2, :].rearrange("p a c -> p (a c)"),
                                         ACT.Copy).then_inc(copied, 1)

            @block.sync
            def _(sp):
                for b in range(QB):
                    sp.wait_ge(copied, b + 1)
                    sp.dma_start(out[0, b * P:(b + 1) * P, :], tok[:, b, :]).then_inc(stored, 16)
                sp.wait_ge(stored, 16 * QB)


def kernel(**inputs):
    import numpy as _np
    import concourse.bacc as _bacc
    from concourse import mybir as _mybir
    from concourse.bass_utils import run_bass_kernel_spmd as _run

    nc = _bacc.Bacc("TRN2", target_bir_lowering=False, num_devices=1)
    arrays, views = {}, {}
    for name, a in inputs.items():
        a = _np.ascontiguousarray(a)
        arrays[f"in_{name}_dram"] = a
        views[name] = nc.dram_tensor(f"in_{name}_dram", a.shape, _mybir.dt.from_np(a.dtype), kind="ExternalInput").ap()
    const = {}
    for name, a in constants().items():
        arrays[f"const_{name}_dram"] = a
        const[name] = nc.dram_tensor(f"const_{name}_dram", a.shape, _mybir.dt.from_np(a.dtype), kind="ExternalInput").ap()
    out = nc.dram_tensor("out_dram", (1, 512, 1024), _mybir.dt.float32, kind="ExternalOutput").ap()
    two_blocks(nc, views, const, out)
    r = _run(nc, [arrays], core_ids=[0])
    return r.results[0]["out_dram"]
```
